# Optimizing a Trainium2 kernel written in Bass

```python
import jax, jax.numpy as jnp
from jax import lax
import numpy as np

D_MODEL = 1024
BATCH = 1
SEQ = 128
DEPTH = 2
DEC_BATCH = 1
DEC_SEQ = 256
PAST_LEN = 128

GRID_W = 64
HEAD_DIM = 64
MIX_WIDTH = D_MODEL
NA_HEADS = MIX_WIDTH // (4 * HEAD_DIM)
GQA_Q_HEADS = MIX_WIDTH // (2 * HEAD_DIM)
GQA_KV_HEADS = GQA_Q_HEADS // 4
GQA_GROUP = GQA_Q_HEADS // GQA_KV_HEADS
FNET_CH = 64
FNET_GROUPS = MIX_WIDTH // (4 * FNET_CH)
NA_WIDTH = NA_HEADS * HEAD_DIM
GQA_WIDTH = GQA_Q_HEADS * HEAD_DIM
KV_WIDTH = GQA_KV_HEADS * HEAD_DIM
FNET_WIDTH = FNET_GROUPS * FNET_CH
IN_SPLITS = (NA_WIDTH, 2 * NA_WIDTH, 3 * NA_WIDTH, 3 * NA_WIDTH + GQA_WIDTH,
             3 * NA_WIDTH + GQA_WIDTH + KV_WIDTH, 3 * NA_WIDTH + GQA_WIDTH + 2 * KV_WIDTH)
IN_WIDTH = IN_SPLITS[-1] + FNET_WIDTH
NA_WIN_H = 8
NA_WIN_W = 16
Q_BLOCK = 128
ROPE_THETA = 10000.0
PEER_HEADS = 8
PEER_NKEYS = 128
PEER_EXPERTS = PEER_NKEYS * PEER_NKEYS
PEER_TOPK = 16
PEER_QDIM = 256
PEER_QHALF = PEER_QDIM // 2
PEER_TOK_BLOCK = 128
ALPHA = (2 * DEPTH) ** 0.25
BETA = (8 * DEPTH) ** -0.25
LN_EPS = 1e-5
RMS_EPS = 1e-6

kernel_name = "hybrid_natten_gqa_fnet_peer_diffusion_step"

def layer_norm(x, g, b):
    xf = x.astype(jnp.float32)
    mu = jnp.mean(xf, axis=-1, keepdims=True)
    var = jnp.mean(jnp.square(xf - mu), axis=-1, keepdims=True)
    return ((xf - mu) * lax.rsqrt(var + LN_EPS) * g + b).astype(x.dtype)

def rms_norm(x, g):
    xf = x.astype(jnp.float32)
    return (xf * lax.rsqrt(jnp.mean(jnp.square(xf), axis=-1, keepdims=True) + RMS_EPS) * g).astype(x.dtype)

def modulation(cond, w_mod, b_mod):
    return jnp.split(jax.nn.silu(cond) @ w_mod + b_mod, 6, axis=-1)

def axial_rope(x, n_tok):
    pos = jnp.arange(n_tok)
    rows = (pos // GRID_W).astype(jnp.float32)
    cols = (pos % GRID_W).astype(jnp.float32)
    half = HEAD_DIM // 2
    quarter = half // 2
    inv = 1.0 / (ROPE_THETA ** (jnp.arange(quarter, dtype=jnp.float32) / quarter))
    shape = (1, n_tok) + (1,) * (x.ndim - 3) + (quarter,)

    def rot(xp, ang):
        cos = jnp.cos(ang).reshape(shape).astype(x.dtype)
        sin = jnp.sin(ang).reshape(shape).astype(x.dtype)
        x1, x2 = xp[..., :quarter], xp[..., quarter:]
        return jnp.concatenate([x1 * cos - x2 * sin, x2 * cos + x1 * sin], axis=-1)

    return jnp.concatenate([rot(x[..., :half], rows[:, None] * inv),
                            rot(x[..., half:], cols[:, None] * inv)], axis=-1)

def blocked_attention(q, k, v):
    b, tq = q.shape[:2]
    nb = tq // Q_BLOCK
    qb = q.reshape((b, nb, Q_BLOCK) + q.shape[2:]).swapaxes(0, 1)
    scale = HEAD_DIM ** -0.5

    def one(qi):
        s = jnp.einsum('bqkgd,bskd->bkgqs', qi, k).astype(jnp.float32) * scale
        p = jax.nn.softmax(s, axis=-1).astype(v.dtype)
        return jnp.einsum('bkgqs,bskd->bqkgd', p, v)

    o = lax.map(one, qb)
    return o.swapaxes(0, 1).reshape(q.shape)

def neighbourhood_attention(qa, ka, va, ctx_k, ctx_v, rpb):
    b, t, h, dh = qa.shape
    rows = t // GRID_W
    kh = min(NA_WIN_H, rows)
    q5 = qa.reshape(b, rows, GRID_W, h, dh)
    k5 = ka.reshape(b, rows, GRID_W, h, dh)
    v5 = va.reshape(b, rows, GRID_W, h, dh)
    row_start = jnp.clip(jnp.arange(rows) - kh // 2, 0, rows - kh)
    col_start = jnp.clip(jnp.arange(GRID_W) - NA_WIN_W // 2, 0, GRID_W - NA_WIN_W)
    col_idx = col_start[:, None] + jnp.arange(NA_WIN_W)
    col_off = col_idx - jnp.arange(GRID_W)[:, None] + (NA_WIN_W - 1)
    rpb_cols = rpb[:, :, col_off]
    scale = HEAD_DIM ** -0.5
    n_win = kh * NA_WIN_W

    def one_row(args):
        r, q_r = args
        rs = row_start[r]
        k_win = lax.dynamic_slice_in_dim(k5, rs, kh, axis=1)[:, :, col_idx]
        v_win = lax.dynamic_slice_in_dim(v5, rs, kh, axis=1)[:, :, col_idx]
        row_off = rs + jnp.arange(kh) - r + (NA_WIN_H - 1)
        bias = rpb_cols[:, row_off].transpose(2, 0, 1, 3)
        s_win = jnp.einsum('bwhd,bjwkhd->bwhjk', q_r, k_win).astype(jnp.float32) * scale + bias[None]
        s_ctx = jnp.einsum('bwhd,blhd->bwhl', q_r, ctx_k).astype(jnp.float32) * scale
        s = jnp.concatenate([s_win.reshape(b, GRID_W, h, n_win), s_ctx], axis=-1)
        p = jax.nn.softmax(s, axis=-1).astype(q_r.dtype)
        p_win = p[..., :n_win].reshape(b, GRID_W, h, kh, NA_WIN_W)
        p_ctx = p[..., n_win:]
        return (jnp.einsum('bwhjk,bjwkhd->bwhd', p_win, v_win)
                + jnp.einsum('bwhl,blhd->bwhd', p_ctx, ctx_v))

    o = lax.map(one_row, (jnp.arange(rows), q5.swapaxes(0, 1)))
    return o.swapaxes(0, 1).reshape(b, t, h * dh)

def fourier_mix(xc, w_f):
    b, t, _ = xc.shape
    xg = xc.reshape(b, t, FNET_GROUPS, FNET_CH).astype(jnp.float32)
    f = jnp.fft.fft2(xg, axes=(1, 3), norm='ortho').real.astype(xc.dtype)
    return jnp.einsum('btgc,gce->btge', f, w_f).reshape(b, t, FNET_WIDTH)

def project(h, w_in, q_gain, k_gain):
    b, t, _ = h.shape
    qa, ka, va, qb, kb, vb, xc = jnp.split(h @ w_in, IN_SPLITS, axis=-1)
    heads = lambda z, n: z.reshape(b, t, n, HEAD_DIM)
    qb = rms_norm(qb.reshape(b, t, GQA_KV_HEADS, GQA_GROUP, HEAD_DIM), q_gain)
    kb = rms_norm(heads(kb, GQA_KV_HEADS), k_gain)
    return (heads(qa, NA_HEADS), heads(ka, NA_HEADS), heads(va, NA_HEADS),
            qb, kb, heads(vb, GQA_KV_HEADS), xc)

def token_mix_context(h, w_in, q_gain, k_gain, w_f, w_out):
    b, t, _ = h.shape
    qa, ka, va, qb, kb, vb, xc = project(h, w_in, q_gain, k_gain)
    oa = blocked_attention(qa[:, :, :, None], ka, va).reshape(b, t, NA_WIDTH)
    ob = blocked_attention(qb, kb, vb).reshape(b, t, GQA_WIDTH)
    oc = fourier_mix(xc, w_f)
    out = jnp.concatenate([oa, ob, oc], axis=-1) @ w_out
    return out, (ka, va, kb, vb)

def token_mix_latent(h, ctx_na_k, ctx_na_v, ctx_gqa_k, ctx_gqa_v, w_in, q_gain, k_gain, rpb, w_f, w_out):
    b, t, _ = h.shape
    qa, ka, va, qb, kb, vb, xc = project(h, w_in, q_gain, k_gain)
    oa = neighbourhood_attention(qa, ka, va, ctx_na_k, ctx_na_v, rpb)
    qb = axial_rope(qb, t)
    kb = axial_rope(kb, t)
    ob = blocked_attention(qb, jnp.concatenate([kb, ctx_gqa_k], axis=1),
                           jnp.concatenate([vb, ctx_gqa_v], axis=1)).reshape(b, t, GQA_WIDTH)
    oc = fourier_mix(xc, w_f)
    return jnp.concatenate([oa, ob, oc], axis=-1) @ w_out

def peer_ffn(h, w_q, sub_keys, u_tab, v_tab):
    b, t, d = h.shape
    xt = h.reshape(-1, d)
    n = xt.shape[0]
    q = (xt @ w_q).reshape(n, PEER_HEADS, 2, PEER_QHALF)
    s = jnp.einsum('nhpc,hpkc->nhpk', q, sub_keys).astype(jnp.float32)
    top_s, top_i = lax.top_k(s, PEER_TOPK)
    cand_s = top_s[:, :, 0, :, None] + top_s[:, :, 1, None, :]
    cand_i = top_i[:, :, 0, :, None] * PEER_NKEYS + top_i[:, :, 1, None, :]
    best_s, best_j = lax.top_k(cand_s.reshape(n, PEER_HEADS, -1), PEER_TOPK)
    experts = jnp.take_along_axis(cand_i.reshape(n, PEER_HEADS, -1), best_j, axis=-1)
    gates = jax.nn.softmax(best_s, axis=-1)
    nb = n // PEER_TOK_BLOCK
    kk = PEER_HEADS * PEER_TOPK
    xb = xt.reshape(nb, PEER_TOK_BLOCK, d)
    eb = experts.reshape(nb, PEER_TOK_BLOCK, kk)
    gb = gates.reshape(nb, PEER_TOK_BLOCK, kk)

    def one(args):
        x_blk, e_blk, g_blk = args
        a = jnp.einsum('tkd,td->tk', u_tab[e_blk], x_blk).astype(jnp.float32)
        w = (g_blk * jax.nn.gelu(a, approximate=False)).astype(x_blk.dtype)
        return jnp.einsum('tk,tkd->td', w, v_tab[e_blk])

    return lax.map(one, (xb, eb, gb)).reshape(b, t, d)

def setup_inputs(seed: int = 0) -> dict:
    key = jax.random.key(seed)
    ks = jax.random.split(key, 28)
    f32 = jnp.float32
    nrm = lambda k, shape, s: jax.random.normal(k, shape, f32) * s
    L, D = DEPTH, D_MODEL
    return {
        "x_prompt": nrm(ks[0], (BATCH, SEQ, D), 1.0),
        "x_sample": nrm(ks[1], (DEC_BATCH, DEC_SEQ, D), 1.0),
        "c": nrm(ks[2], (DEC_BATCH, D), 1.0),
        "cache_na_k": nrm(ks[3], (DEC_BATCH, L, PAST_LEN, NA_HEADS, HEAD_DIM), 1.0),
        "cache_na_v": nrm(ks[4], (DEC_BATCH, L, PAST_LEN, NA_HEADS, HEAD_DIM), 1.0),
        "cache_gqa_k": nrm(ks[5], (DEC_BATCH, L, PAST_LEN, GQA_KV_HEADS, HEAD_DIM), 1.0),
        "cache_gqa_v": nrm(ks[6], (DEC_BATCH, L, PAST_LEN, GQA_KV_HEADS, HEAD_DIM), 1.0),
        "c_ctx": nrm(ks[7], (D,), 1.0),
        "w_in": nrm(ks[8], (L, D, IN_WIDTH), D ** -0.5),
        "q_gain": 1.0 + nrm(ks[9], (L, HEAD_DIM), 0.02),
        "k_gain": 1.0 + nrm(ks[10], (L, HEAD_DIM), 0.02),
        "na_rpb": nrm(ks[11], (L, NA_HEADS, 2 * NA_WIN_H - 1, 2 * NA_WIN_W - 1), 0.1),
        "w_fourier": nrm(ks[12], (L, FNET_GROUPS, FNET_CH, FNET_CH), FNET_CH ** -0.5),
        "w_out": nrm(ks[13], (L, MIX_WIDTH, D), BETA * MIX_WIDTH ** -0.5),
        "w_mod": nrm(ks[14], (L, D, 6 * D), D ** -0.5),
        "b_mod": nrm(ks[15], (L, 6 * D), 0.02),
        "ln1_g": 1.0 + nrm(ks[16], (L, D), 0.02),
        "ln1_b": nrm(ks[17], (L, D), 0.02),
        "ln2_g": 1.0 + nrm(ks[18], (L, D), 0.02),
        "ln2_b": nrm(ks[19], (L, D), 0.02),
        "peer_wq": nrm(ks[20], (L, D, PEER_HEADS * PEER_QDIM), D ** -0.5),
        "peer_subkeys": nrm(ks[21], (L, PEER_HEADS, 2, PEER_NKEYS, PEER_QHALF), PEER_QHALF ** -0.5),
        "peer_u": nrm(ks[22], (L, PEER_EXPERTS, D), D ** -0.5),
        "peer_v": nrm(ks[23], (L, PEER_EXPERTS, D), BETA),
    }

def reference(x_prompt, x_sample, c, cache_na_k, cache_na_v, cache_gqa_k, cache_gqa_v, c_ctx,
              w_in, q_gain, k_gain, na_rpb, w_fourier, w_out, w_mod, b_mod,
              ln1_g, ln1_b, ln2_g, ln2_b, peer_wq, peer_subkeys, peer_u, peer_v):
    yp, ys = x_prompt, x_sample
    na_k, na_v, gqa_k, gqa_v = [], [], [], []
    for l in range(DEPTH):
        proj = (w_in[l], q_gain[l], k_gain[l])
        ffn = (peer_wq[l], peer_subkeys[l], peer_u[l], peer_v[l])
        sh1, sc1, g1, sh2, sc2, g2 = modulation(c_ctx, w_mod[l], b_mod[l])
        mix, (ka, va, kb, vb) = token_mix_context(yp * (1 + sc1) + sh1, *proj, w_fourier[l], w_out[l])
        yp = layer_norm(ALPHA * yp + g1 * mix, ln1_g[l], ln1_b[l])
        yp = layer_norm(ALPHA * yp + g2 * peer_ffn(yp * (1 + sc2) + sh2, *ffn), ln2_g[l], ln2_b[l])
        na_k.append(ka)
        na_v.append(va)
        gqa_k.append(kb)
        gqa_v.append(vb)
        sh1, sc1, g1, sh2, sc2, g2 = modulation(c[:, None, :], w_mod[l], b_mod[l])
        mix = token_mix_latent(ys * (1 + sc1) + sh1, cache_na_k[:, l], cache_na_v[:, l],
                               cache_gqa_k[:, l], cache_gqa_v[:, l], *proj, na_rpb[l],
                               w_fourier[l], w_out[l])
        ys = layer_norm(ALPHA * ys + g1 * mix, ln1_g[l], ln1_b[l])
        ys = layer_norm(ALPHA * ys + g2 * peer_ffn(ys * (1 + sc2) + sh2, *ffn), ln2_g[l], ln2_b[l])
    return (yp, ys, jnp.stack(na_k, axis=1), jnp.stack(na_v, axis=1),
            jnp.stack(gqa_k, axis=1), jnp.stack(gqa_v, axis=1))


_drawn_inputs = setup_inputs


def setup_inputs(seed=0):
    import zlib

    import numpy as np

    out = dict(_drawn_inputs(seed))
    spreads = {}
    factors = {'q_gain': 8.0, 'na_rpb': 5.12}
    for name, (base, spread) in spreads.items():
        noise = np.random.default_rng([zlib.crc32(name.encode()), seed]).standard_normal(out[name].shape)
        drawn = base * np.exp(spread * noise) if base else spread * noise
        out[name] = __import__('jax').numpy.asarray(drawn.astype(out[name].dtype))
    for name, factor in factors.items():
        out[name] = (out[name] * factor).astype(out[name].dtype)
    return out
```

```python
from contextlib import ExitStack

import concourse.bass as bass
from concourse import mybir

F32 = mybir.dt.float32
BF16 = mybir.dt.bfloat16
U32 = mybir.dt.uint32
ALU = mybir.AluOpType
ACT = mybir.ActivationFunctionType
AX = mybir.AxisListType

P = 128
DEPTH = 2
D = 1024
NC = D // P
HD = 64
NA_H, Q_H, KV_H = 4, 8, 2
NA_Q, NA_K, NA_V, G_Q = 0, 256, 512, 768
G_K, G_V, FN = 1280, 1408, 1536
IN_W = 1792
RMS_HEADS = Q_H + KV_H
GRID_W = 64
EXPERTS = 16384
R_H, TOPK, KEYS = 8, 16, 128
PER_TOKEN = R_H * TOPK
ALPHA = (2 * DEPTH) ** 0.25
LN_EPS, RMS_EPS = 1e-5, 1e-6
SCALE = HD ** -0.5
LOWEST = -3.0e38

TW = 256
WSLOTS = 3
G = 8
GROUPS = PER_TOKEN // G
DIAGS = 4

MIXES = [(0, 0), (0, 1), (1, 0), (1, 1)]
BLOCKS = [[0], [1, 2], [3], [4, 5]]
PART_SH1, PART_SC1, PART_G1, PART_SH2, PART_SC2, PART_G2 = range(6)


def modulation_steps(l):
    return [("mod", l, c) for c in range(6)]


def mix_steps(m):
    l, latent = MIXES[m]
    qs = BLOCKS[m]
    steps = [("bias", l)] if latent else []
    steps += [("xT", q) for q in qs]
    steps += [("proj", m, n) for n in range(IN_W // TW)]
    steps += [("norm", q) for q in qs]
    steps += [("qkT", q) for q in qs]
    for q in qs:
        steps += [("att", q, u, u + 2) for u in range(0, 6, 2)]
    steps += [("four", m)]
    steps += [] if latent else [("kvout", qs[0])]
    steps += [("oT", q) for q in qs]
    steps += [("gate", m)]
    steps += [("outp", m, n) for n in range(D // TW)]
    for q in qs:
        steps += [("ln1", q), ("h2", q)]
    steps += [("wq", m, n) for n in range(R_H + 1)]
    for q in qs:
        steps += [("top", q, 0), ("top", q, 8), ("pick", q)]
    return steps


def beside(q, steps):
    out, at = [], 0
    for n, step in enumerate(steps):
        until = min(GROUPS, ((n + 1) * GROUPS) // (len(steps) + 1))
        if until > at:
            out.append(("gather", q, at, until))
            at = until
        out.append(step)
    out.append(("gather", q, at, GROUPS))
    return out


def build_schedule():
    first = mix_steps(0)
    ln1 = first.index(("ln1", 0))
    gate = first.index(("gate", 0))
    mods = modulation_steps(0)
    s = mods[:2] + first[:gate] + [mods[2]] + first[gate:ln1 + 1] + mods[3:5] + first[ln1 + 1:]
    s += beside(0, [mods[5]] + mix_steps(1))
    s += beside(1, [("ln2", 0)] + modulation_steps(1) + mix_steps(2))
    s += [("ln2", 1)] + beside(2, []) + [("ln2", 2)]
    s += beside(3, mix_steps(3))
    s += [("ln2", 3)] + beside(4, []) + [("ln2", 4)] + beside(5, []) + [("ln2", 5)]
    return s


SCHEDULE = build_schedule()


def rounds_of(step):
    kind, a = step[0], step[1:]
    if kind == "mod":
        return [("MD",) + a] + ([("MC",) + a] if a[1] not in (PART_G1, PART_G2) else [])
    if kind == "bias":
        return [("B", a[0], 0), ("B", a[0], 1)]
    if kind == "xT":
        return [("X", a[0])]
    if kind == "proj":
        return [("J",) + a]
    if kind == "qkT":
        return [("T0", a[0]), ("T1", a[0])]
    if kind == "att":
        q, u0, u1 = a
        out = [("A", q, u0)]
        for u in range(u0, u1):
            out += ([("A", q, u + 1)] if u + 1 < u1 else []) + [("PT", q, u), ("O", q, u)]
        return out
    if kind == "four":
        qs = BLOCKS[a[0]]
        return [("FY", q) for q in qs] + [("FF", a[0])] + [("FO", q) for q in qs]
    if kind == "oT":
        return [("OT", a[0])]
    if kind == "gate":
        return [("G", BLOCKS[a[0]][0], 1)]
    if kind == "outp":
        return [("Z", q) for q in BLOCKS[a[0]]] if a[1] == 0 else []
    if kind == "h2":
        return [("X2", a[0]), ("H2", a[0])]
    if kind == "wq":
        m, n = a
        return ([("WQ", m, n)] if n < R_H else []) + ([("SC", m, n - 1)] if n else [])
    if kind == "ln2":
        return [("G", a[0], 2)]
    return []


ROUNDS = [r for s in SCHEDULE for r in rounds_of(s)]
PAIRS = 3
ROUND = {r: n for n, r in enumerate(ROUNDS)}
BY_DVE = {"MD", "MC", "B", "O", "Z"}
BY_TILE = {"MD", "J", "Z", "SC"}


def numbered(kinds, keys):
    return {k: n + 1 for n, k in enumerate(k for s in SCHEDULE if s[0] in kinds for k in keys(s))}


def counted(rounds):
    return {r: n + 1 for n, r in enumerate(rounds)}


DRAINED_BY_DVE = counted(r for r in ROUNDS if r[0] in BY_DVE)
DRAINED_BY_ACT = counted(r for r in ROUNDS if r[0] not in BY_DVE)
FILLED = counted(r for r in ROUNDS if r[0] not in BY_TILE)
LN = numbered(("ln1", "ln2"), lambda s: [(s[1], 1 if s[0] == "ln1" else 2)])
NORM = numbered(("norm",), lambda s: [s[1]])
ROOTS = numbered(("norm", "ln1", "ln2"), lambda s: [(s[0], s[1])])
UNIT = numbered(("att",), lambda s: [(s[1], u) for u in range(s[2], s[3])])
ROUTE = numbered(("pick",), lambda s: [s[1]])
MOD = numbered(("mod",), lambda s: [s[1:]])
MOD_COLS = [k for k in MOD if k[1] not in (PART_G1, PART_G2)]
TILES = numbered(("mod", "proj", "outp", "wq"),
                 lambda s: [s + (t,) for t in range(4)] if s[0] == "mod" else [] if s[0] == "wq" and s[2] == R_H else [s])


def ln_before(step):
    return sum(s[0] in ("ln1", "ln2") for s in SCHEDULE[:SCHEDULE.index(step)])


def routes_before(step):
    return sum(s[0] == "pick" for s in SCHEDULE[:SCHEDULE.index(step)])


def mix_of(q):
    return next(m for m in range(4) if q in BLOCKS[m])


def place_in_mix(q):
    return q - BLOCKS[mix_of(q)][0]


def width(m):
    return P * len(BLOCKS[m])


def last_tile(key):
    kind = key[0]
    if kind == "MD":
        return ("mod",) + key[1:] + (3,)
    if kind == "Z":
        return ("outp", mix_of(key[1]), 3)
    return ({"J": "proj", "SC": "wq"}[kind],) + key[1:]


def tile_arrival(key):
    n = TILES[key]
    slot = (n - 1) % WSLOTS
    return slot, 16 * sum(2 if k[0] == "wq" else 1 for k, v in TILES.items() if (v - 1) % WSLOTS == slot and v <= n)


CONST = {}
_at = 0
for _name, _n in (("ident", P), ("sel", 2 * P), ("rope", 2 * 2 * HD), ("dft_ctx", 2 * P), ("dft_lat", 2 * 2 * 2 * P),
                  ("dft_ch", 2 * P), ("window", GRID_W), ("shift", 2 * GRID_W), ("iota", TOPK), ("zero", P)):
    CONST[_name] = (_at, _at + _n)
    _at += _n
CONST_W = _at
RPB_ROWS, RPB_COLS = 15, 31
ROW_DIFFS = 7


def hybrid_step(nc, i, o):
    ctx = ExitStack()
    with ctx:
        def sb(name, shape, dt=F32):
            return ctx.enter_context(nc.sbuf_tensor(name, shape, dt))

        def sem(name):
            return ctx.enter_context(nc.semaphore(name))

        u_rows = sb("u_rows", [P, G, D])
        v_rows = sb("v_rows", [P, G, D])
        wtiles = sb("wtiles", [P, WSLOTS, NC, TW])
        sktiles = sb("sktiles", [P, WSLOTS, 2, KEYS])
        x_tok = sb("x_tok", [P, 3, D])
        h_tok = sb("h_tok", [P, 3, D])
        hT = sb("hT", [P, NC, 2 * P])
        mod_rows = sb("mod_rows", [66, 2, D])
        mod_cols = sb("mod_cols", [P, DEPTH, 4, NC, 2])
        rows = sb("rows", [P, 2 * D])
        ln_rows = rows[:, :].rearrange("p (r n) -> p r n", r=2)
        bias = rows[:, :].rearrange("p (b h n) -> p b h n", b=2, h=NA_H)
        arena = sb("arena", [P, 7424])
        qT = sb("qT", [P, 6, 2 * P])
        kT = sb("kT", [P, 3, 3 * P])
        consts = sb("consts", [P, CONST_W])
        rpb = sb("rpb", [RPB_COLS, DEPTH, NA_H, RPB_ROWS])
        gains = sb("gains", [P, DEPTH, 2, HD])
        wf = sb("wf", [P, DEPTH, 2, P])
        v_ctx = sb("v_ctx", [P, (NA_H + KV_H) * HD])
        cond = sb("cond", [P, NC, 2])
        cond_e = sb("cond_e", [P, NC, 2])
        cond_s = sb("cond_s", [P, NC, 2])
        stats = sb("stats", [P, 2, 6])
        mean_var = sb("mean_var", [P, 2])
        root_in = sb("root_in", [P, RMS_HEADS])
        root = sb("root", [P, RMS_HEADS])
        rroot = sb("rroot", [P, RMS_HEADS])
        maxes = sb("maxes", [P, 2])
        neg_max = sb("neg_max", [P, 2, 2])
        row_sum = sb("row_sum", [P, 2, 2])
        inv_sum = sb("inv_sum", [P, 2])
        top_s = sb("top_s", [P, 2 * R_H, TOPK])
        top_i = sb("top_i", [P, 2 * R_H, TOPK], U32)
        best_s = sb("best_s", [P, R_H, TOPK])
        best_j = sb("best_j", [P, R_H, TOPK], U32)
        half_j = sb("half_j", [P, PER_TOKEN], U32)
        half_f = sb("half_f", [P, PER_TOKEN])
        picked = sb("picked", [P, 2, PER_TOKEN])
        gate_e = sb("gate_e", [P, R_H, TOPK])
        gate_n = sb("gate_n", [P, R_H])
        experts = sb("experts", [P, 3, PER_TOKEN], U32)
        gates = sb("gates", [P, 3, PER_TOKEN])
        products = sb("products", [P, D], BF16)
        u_index = sb("u_index", [P, 2, G], U32)
        v_index = sb("v_index", [P, 2, G], U32)
        dots = sb("dots", [P, G])
        gelu = sb("gelu", [P, G])
        weight = sb("weight", [P, G])
        diag = sb("diag", [P, DIAGS, P])
        qkv = arena[:, 0:2 * IN_W].rearrange("p (b n) -> p b n", b=2)
        probs = arena[:, 3584:5120].rearrange("p (a i n) -> p a i n", a=2, i=2)
        pT = arena[:, 5120:5888].rearrange("p (i n) -> p i n", i=2)
        fy = arena[:, 5888:6912].rearrange("p (b n) -> p b n", b=2)
        fT = arena[:, 6912:7424].rearrange("p (g n) -> p g n", g=2)
        squares = arena[:, 3584:3584 + RMS_HEADS * HD]
        turned = arena[:, 3584 + 640:3584 + 1280]
        turned2 = arena[:, 3584 + 1280:3584 + 1920]
        gate_b = arena[:, 3584:3584 + D].rearrange("p (a n) -> p a n", a=2)
        z = arena[:, 4608:4608 + D]
        scores = arena[:, 0:2 * 2048].rearrange("p (b n) -> p b n", b=2)
        cand = arena[:, 4096:6144]
        qpT = arena[:, 6144:6144 + 1024].rearrange("p (a i n) -> p a i n", a=2, i=2)

        def const(name):
            a, b = CONST[name]
            return consts[:, a:b]

        ident = const("ident")
        sel = const("sel").rearrange("p (c n) -> p c n", c=2)
        rope = const("rope").rearrange("p (b f n) -> p b f n", b=2, f=2)
        dft_ctx = const("dft_ctx").rearrange("p (f n) -> p f n", f=2)
        dft_lat = const("dft_lat").rearrange("p (b f n) -> p b f n", b=2, f=2)
        dft_ch = const("dft_ch")
        window = const("window")
        shift = const("shift")
        iota = const("iota")

        acc = ctx.enter_context(nc.psum_tensor("acc", [P, 2, 512], F32))
        pairs = [ctx.enter_context(nc.psum_tensor(f"pair{n}", [P, 2, 512], F32)) for n in range(PAIRS)]

        consts_landed = sem("consts_landed")
        x_landed = sem("x_landed")
        w_landed = [sem(f"w_landed{n}") for n in range(WSLOTS)]
        w_used = sem("w_used")
        b_landed = [sem(f"b_landed{n}") for n in range(2)]
        ln_rows_landed = sem("ln_rows_landed")
        ctx_landed = sem("ctx_landed")
        kv_stored = sem("kv_stored")
        y_stored = sem("y_stored")
        filled = sem("filled")
        drained_by_act = sem("drained_by_act")
        drained_by_dve = sem("drained_by_dve")
        cond_exp = sem("cond_exp")
        cond_ready = sem("cond_ready")
        squares_ready = sem("squares_ready")
        root_in_ready = sem("root_in_ready")
        root_ready = sem("root_ready")
        norm_ready = sem("norm_ready")
        neg_max_ready = sem("neg_max_ready")
        ln_done = sem("ln_done")
        best_ready = sem("best_ready")
        gate_exp = sem("gate_exp")
        route_ready = sem("route_ready")
        acc_drained = sem("acc_drained")
        index_copied = sem("index_copied")
        issue_granted = sem("issue_granted")
        u_landed = [sem(f"u_landed{n}") for n in range(G)]
        v_landed = [sem(f"v_landed{n}") for n in range(G)]
        u_used = sem("u_used")
        v_used = sem("v_used")
        gelu_ready = sem("gelu_ready")
        weight_ready = sem("weight_ready")
        diag_ready = sem("diag_ready")
        dve_chain = sem("dve_chain")
        act_chain = sem("act_chain")

        N_CONST_DMAS = 5

        def pair(key):
            return pairs[ROUND[key] % PAIRS]

        def wait_filled(eng, key):
            if key[0] in BY_TILE:
                eng.wait_ge(w_used, TILES[last_tile(key)])
            else:
                eng.wait_ge(filled, FILLED[key])
            return pair(key)

        def wait_drained(eng, key):
            if key[0] in BY_DVE:
                eng.wait_ge(drained_by_dve, DRAINED_BY_DVE[key])
            else:
                eng.wait_ge(drained_by_act, DRAINED_BY_ACT[key])

        block = ctx.enter_context(nc.Block())

        @block.sync
        def _(sp):
            sp.dma_start(consts[:, :], i["consts"]).then_inc(consts_landed, 16)
            sp.dma_start(cond[:, :, :], i["cond"]).then_inc(consts_landed, 16)
            for b, src in enumerate((i["x_prompt"][0], i["x_sample"][0, 0:P], i["x_sample"][0, P:2 * P])):
                sp.dma_start(x_tok[:, b, :], src).then_inc(x_landed, 16)
            sp.dma_start(rpb[:, :, :, :], i["rpb"]).then_inc(consts_landed, 16)
            sp.dma_start(gains[:, :, :, :], i["gains"].partition_broadcast(P)).then_inc(consts_landed, 16)
            sp.dma_start(wf[:, :, :, :], i["wf"]).then_inc(consts_landed, 16)

            def weights(key, src):
                n = TILES[key]
                slot = (n - 1) % WSLOTS
                if n > WSLOTS:
                    sp.wait_ge(w_used, n - WSLOTS)
                sp.dma_start(wtiles[:, slot, :, :], src).then_inc(w_landed[slot], 16)
                return slot

            def cols(w, l, n):
                return w[l, :, n * TW:(n + 1) * TW].rearrange("(c p) n -> p c n", p=P)

            for step in SCHEDULE:
                kind, a = step[0], step[1:]
                if kind == "mod":
                    l, c = a
                    if c in (PART_G1, PART_G2):
                        dst = mod_rows[32 * l:32 * l + 2, c // PART_G2, :]
                    else:
                        n = MOD_COLS.index(a)
                        dst = mod_rows[64:66, n % 2, :]
                        if n >= 2:
                            wait_filled(sp, ("MC",) + MOD_COLS[n - 2])
                    if MOD[a] > 2:
                        wait_drained(sp, ("MD",) + list(MOD)[MOD[a] - 3])
                    sp.dma_start(dst, i["b_mod"][l, c * D:(c + 1) * D].partition_broadcast(2))\
                        .then_inc(b_landed[(MOD[a] - 1) % 2], 16)
                    for t in range(4):
                        weights(step + (t,), cols(i["w_mod"], l, 4 * c + t))
                elif kind == "proj":
                    weights(step, cols(i["w_in"], MIXES[a[0]][0], a[1]))
                elif kind == "outp":
                    weights(step, cols(i["w_out"], MIXES[a[0]][0], a[1]))
                elif kind == "wq" and a[1] < R_H:
                    l = MIXES[a[0]][0]
                    slot = weights(step, cols(i["peer_wq"], l, a[1]))
                    sp.dma_start(sktiles[:, slot, :, :], i["sub_keys"][l, :, 2 * a[1]:2 * a[1] + 2, :])\
                        .then_inc(w_landed[slot], 16)
                elif kind == "bias":
                    l = a[0]
                    if l:
                        wait_filled(sp, ("O", 2, 5))
                    sp.dma_start(kT[:, :, 2 * P:3 * P], i["ctx_kT"][l]).then_inc(ctx_landed, 16)
                    sp.dma_start(v_ctx[:, :], i["ctx_v"][l]).then_inc(ctx_landed, 16)
                elif kind in ("ln1", "ln2"):
                    which = 1 if kind == "ln1" else 2
                    n, l = LN[(a[0], which)], a[0] // 3
                    if n > 1:
                        sp.wait_ge(ln_done, n - 1)
                    if which == 1 and MIXES[mix_of(a[0])][1]:
                        wait_filled(sp, ("O", BLOCKS[mix_of(a[0])][-1], 5))
                    for r, name in enumerate((f"ln{which}_g", f"ln{which}_b")):
                        sp.dma_start(ln_rows[:, r, :], i[name][l, :].partition_broadcast(P))\
                            .then_inc(ln_rows_landed, 16)
                    if kind == "ln2" and l == DEPTH - 1:
                        sp.wait_ge(ln_done, n)
                        dst = o["y_prompt"][0] if a[0] == 3 else o["y_sample"][0, (a[0] - 4) * P:(a[0] - 3) * P]
                        sp.dma_start(dst, x_tok[:, a[0] % 3, :]).then_inc(y_stored, 16)
                elif kind == "kvout":
                    q = a[0]
                    l = q // 3
                    sp.wait_ge(norm_ready, NORM[q])
                    for name, at, n in (("new_na_k", NA_K, 256), ("new_na_v", NA_V, 256),
                                        ("new_gqa_k", G_K, 128), ("new_gqa_v", G_V, 128)):
                        sp.dma_start(o[name][l], qkv[:, 0, at:at + n]).then_inc(kv_stored, 16)
            sp.wait_ge(kv_stored, 16 * 8)
            sp.wait_ge(y_stored, 16 * 3)

        @block.gpsimd
        def _(pool):
            def gather_u(group, j, half):
                pool.wait_ge(u_used, group * G + j + 1)
                pool.sem_inc(issue_granted, 1)
                pool.indirect_dma_start(
                    out=u_rows[:, j, :], out_offset=None, in_=i["peer_u"],
                    in_offset=bass.IndirectOffsetOnAxis(ap=u_index[:, half, j:j + 1], axis=0),
                ).then_inc(u_landed[j], 16)

            def gather_v(group, j, half):
                pool.wait_ge(v_used, group * G + j + 1)
                pool.sem_inc(issue_granted, 1)
                pool.indirect_dma_start(
                    out=v_rows[:, j, :], out_offset=None, in_=i["peer_v"],
                    in_offset=bass.IndirectOffsetOnAxis(ap=v_index[:, half, j:j + 1], axis=0),
                ).then_inc(v_landed[j], 16)

            def phase(q, g, half, with_u=True, with_v=True):
                if with_u:
                    pool.tensor_copy(u_index[:, half, :], experts[:, q % 3, bass.ds(g * G, G)]).then_inc(index_copied, 1)
                if with_v:
                    pool.tensor_copy(v_index[:, 1 - half, :], experts[:, q % 3, bass.ds(g * G - G, G)])\
                        .then_inc(index_copied, 1)
                pool.wait_ge(index_copied, q * 2 * GROUPS + g * 2 + (1 if with_u else 0))
                for j in range(G):
                    if with_u:
                        gather_u(g + q * GROUPS, j, half)
                    if with_v:
                        gather_v(g + q * GROUPS - 1, j, 1 - half)

            for q in range(6):
                pool.wait_ge(route_ready, ROUTE[q])
                phase(q, 0, 0, with_v=False)
                with pool.Fori(1, GROUPS - 1, 2) as g:
                    phase(q, g, 1)
                    phase(q, g + 1, 0)
                phase(q, GROUPS - 1, 1)
                phase(q, GROUPS, 0, with_u=False)

        @block.tensor
        def _(pe):
            def open_round(key):
                if ROUND[key] >= PAIRS:
                    wait_drained(pe, ROUNDS[ROUND[key] - PAIRS])
                return pair(key)

            def tile(key):
                slot, n = tile_arrival(key)
                pe.wait_ge(w_landed[slot], n)
                return wtiles[:, slot, :, :]

            def transpose8(dst, src):
                for c in range(NC):
                    last = nc.tensor.transpose(dst[:, c // 4, (c % 4) * P:(c % 4 + 1) * P], src(c), ident)
                return last

            def scores_round(q, u):
                m, b = mix_of(q), place_in_mix(q)
                nk = 3 * P if MIXES[m][1] else P
                dst = open_round(("A", q, u))
                kp = min(u, 2)
                for h in range(2):
                    rows = slice(64 * h, 64 * h + 64)
                    last = nc.tensor.matmul(dst[:, h, 0:nk], qT[rows, u, b * P:(b + 1) * P], kT[rows, kp, 0:nk],
                                            start=True, stop=True)
                last.then_inc(filled, 1)

            def attention(q, u0, u1):
                m = mix_of(q)
                b, latent = place_in_mix(q), MIXES[m][1]
                chunks = 3 if latent else 1
                wait_drained(pe, ("T1", BLOCKS[m][-1]))
                if latent:
                    pe.wait_ge(ctx_landed, 32 * (q // 3 + 1))
                scores_round(q, u0)
                for u in range(u0, u1):
                    if u + 1 < u1:
                        scores_round(q, u + 1)
                    dst = open_round(("PT", q, u))
                    wait_drained(pe, ("A", q, u))
                    for h in range(2):
                        for k in range(chunks):
                            last = nc.tensor.transpose(dst[:, h, k * P:(k + 1) * P], probs[:, u % 2, h, k * P:(k + 1) * P], ident)
                    last.then_inc(filled, 1)
                    dst = open_round(("O", q, u))
                    wait_drained(pe, ("PT", q, u))
                    for h in range(2):
                        own = (NA_V + (2 * u + h) * HD) if u < 2 else (G_V + h * HD)
                        old = ((2 * u + h) * HD) if u < 2 else (256 + h * HD)
                        for k in range(chunks):
                            v = v_ctx[:, old:old + HD] if k == 2 else qkv[:, k, own:own + HD]
                            last = nc.tensor.matmul(dst[:, 0, h * HD:(h + 1) * HD], pT[:, h, k * P:(k + 1) * P], v,
                                                    start=(k == 0), stop=(k == chunks - 1))
                    last.then_inc(filled, 1)

            def fourier(m):
                l, latent = MIXES[m]
                qs = BLOCKS[m]
                t = width(m)
                for b, q in enumerate(qs):
                    dst = open_round(("FY", q))
                    for g in range(2):
                        last = nc.tensor.matmul(dst[:, 0, g * 256:(g + 1) * 256], hT[:, g, b * P:(b + 1) * P], dft_ch,
                                                start=True, stop=True)
                    last.then_inc(filled, 1)
                dst = open_round(("FF", m))
                wait_drained(pe, ("FY", qs[-1]))
                for g in range(2):
                    for b in range(len(qs)):
                        for f in range(2):
                            table = dft_lat[:, b, f, :] if latent else dft_ctx[:, f, :]
                            last = nc.tensor.matmul(dst[:, g, 0:t], fy[:, b, g * 256 + f * P:g * 256 + (f + 1) * P], table,
                                                    start=(b == 0 and f == 0), stop=(b == len(qs) - 1 and f == 1))
                last.then_inc(filled, 1)
                for b, q in enumerate(qs):
                    dst = open_round(("FO", q))
                    wait_drained(pe, ("FF", m))
                    for g in range(2):
                        last = nc.tensor.matmul(dst[:, 0, g * P:(g + 1) * P], fT[:, g, b * P:(b + 1) * P], wf[:, l, g, :],
                                                start=True, stop=True)
                    last.then_inc(filled, 1)

            def experts_sum(q, g0, g1):
                if g0 == 0:
                    if q:
                        pe.wait_ge(acc_drained, q)
                    else:
                        pe.sem_inc(v_used, G)
                    for half in range(2):
                        nc.tensor.matmul(acc[:, half, :], const("zero")[0:1, :], consts[0:1, 0:512], start=True, stop=True)
                base = q * GROUPS
                with pe.Fori(base + g0, base + g1) as g:
                    for j in range(G):
                        pe.wait_ge(diag_ready, g * G + j + 1)
                        pe.wait_ge(v_landed[j], g * 16 + 16)
                        for half in range(2):
                            last = nc.tensor.matmul(acc[:, half, :], diag[:, j % DIAGS, :],
                                                    v_rows[:, j, half * 512:(half + 1) * 512],
                                                    start=False, stop=True, skip_group_check=True)
                        last.then_inc(v_used, 1)

            pe.wait_ge(consts_landed, 16 * N_CONST_DMAS)
            for step in SCHEDULE:
                kind, a = step[0], step[1:]
                if kind == "gather":
                    experts_sum(*a)
                elif kind == "mod":
                    l, c = a
                    at = 32 * l if c in (PART_G1, PART_G2) else 64
                    dst = open_round(("MD",) + a)
                    pe.wait_ge(cond_ready, 1)
                    for t in range(4):
                        w = tile(step + (t,))
                        for k in range(NC):
                            last = nc.tensor.matmul(dst[at:at + 2, t // 2, (t % 2) * TW:(t % 2 + 1) * TW], cond_s[:, k, :],
                                                    w[:, k, :], start=(k == 0), stop=(k == NC - 1))
                        last.then_inc(w_used, 1)
                    if c not in (PART_G1, PART_G2):
                        dst = open_round(("MC",) + a)
                        wait_drained(pe, ("MD",) + a)
                        for k in range(NC):
                            last = nc.tensor.transpose(dst[:, 0, 2 * k:2 * k + 2], mod_rows[64:66, MOD_COLS.index(a) % 2, k * P:(k + 1) * P],
                                                       ident[64:66, 64:66])
                        last.then_inc(filled, 1)
                elif kind == "bias":
                    l = a[0]
                    for half in range(2):
                        dst = open_round(("B", l, half))
                        for c in range(32):
                            key_col = 32 * half + c
                            pick = shift[0:RPB_COLS, 63 - key_col:127 - key_col]
                            at = (c % 16) * NA_H * ROW_DIFFS
                            for row in range(2):
                                out = dst[64 * row:64 * row + 64, c // 16, at:at + NA_H * ROW_DIFFS]
                                last = nc.tensor.matmul(out.rearrange("p (h r) -> p h r", h=NA_H), pick,
                                                        rpb[:, l, :, 4:4 + ROW_DIFFS], start=True, stop=True)
                        last.then_inc(filled, 1)
                elif kind == "xT":
                    q = a[0]
                    dst = open_round(("X", q))
                    if q < 3:
                        pe.wait_ge(x_landed, 48)
                    else:
                        pe.wait_ge(ln_done, LN[(q - 3, 2)])
                    transpose8(dst, lambda c: x_tok[:, q % 3, c * P:(c + 1) * P]).then_inc(filled, 1)
                elif kind in ("proj", "outp"):
                    m, n = a
                    w = tile(step)
                    if n == 0:
                        for q in BLOCKS[m]:
                            wait_drained(pe, ("X" if kind == "proj" else "OT", q))
                    if kind == "proj":
                        both = open_round(("J", m, n))
                    for b, q in enumerate(BLOCKS[m]):
                        if kind == "outp":
                            dst = open_round(("Z", q)) if n == 0 else pair(("Z", q))
                            dst = dst[:, n // 2, (n % 2) * TW:(n % 2 + 1) * TW]
                        else:
                            dst = both[:, b, 0:TW]
                        for k in range(NC):
                            last = nc.tensor.matmul(dst, hT[:, k, b * P:(b + 1) * P], w[:, k, :],
                                                    start=(k == 0), stop=(k == NC - 1))
                    last.then_inc(w_used, 1)
                elif kind == "qkT":
                    q = a[0]
                    b = place_in_mix(q)
                    src = qkv[:, b, :]
                    dst = open_round(("T0", q))
                    pe.wait_ge(norm_ready, NORM[q])
                    wait_drained(pe, ("J", mix_of(q), IN_W // TW - 1))
                    parts = [src[:, NA_Q + k * P:NA_Q + (k + 1) * P] for k in range(2)]
                    parts += [src[:, G_Q + k * P:G_Q + (k + 1) * P] for k in range(4)]
                    parts += [src[:, NA_K + k * P:NA_K + (k + 1) * P] for k in range(2)]
                    transpose8(dst, lambda c: parts[c]).then_inc(filled, 1)
                    dst = open_round(("T1", q))
                    for k, at in enumerate((G_K, FN, FN + P)):
                        last = nc.tensor.transpose(dst[:, 0, k * P:(k + 1) * P], src[:, at:at + P], ident)
                    last.then_inc(filled, 1)
                elif kind == "att":
                    attention(*a)
                elif kind == "four":
                    fourier(a[0])
                elif kind == "oT":
                    q = a[0]
                    b = place_in_mix(q)
                    dst = open_round(("OT", q))
                    wait_drained(pe, ("O", q, 5))
                    wait_drained(pe, ("FO", q))
                    at = [NA_Q, NA_Q + P, G_Q, G_Q + P, G_Q + 2 * P, G_Q + 3 * P, FN, FN + P]
                    transpose8(dst, lambda c: qkv[:, b, at[c]:at[c] + P]).then_inc(filled, 1)
                elif kind in ("gate", "ln2"):
                    q, which = (BLOCKS[a[0]][0], 1) if kind == "gate" else (a[0], 2)
                    l, latent = q // 3, int(q % 3 > 0)
                    dst = open_round(("G", q, which))
                    wait_drained(pe, ("MD", l, PART_G1 if which == 1 else PART_G2))
                    for half in range(2):
                        last = nc.tensor.matmul(dst[:, half, :], sel[32 * l:32 * l + 2, latent, :],
                                                mod_rows[32 * l:32 * l + 2, which - 1, half * 512:(half + 1) * 512],
                                                start=True, stop=True)
                    last.then_inc(filled, 1)
                elif kind == "h2":
                    q = a[0]
                    b = place_in_mix(q)
                    dst = open_round(("X2", q))
                    pe.wait_ge(ln_done, LN[(q, 1)])
                    transpose8(dst, lambda c: x_tok[:, q % 3, c * P:(c + 1) * P]).then_inc(filled, 1)
                    dst = open_round(("H2", q))
                    wait_drained(pe, ("X2", q))
                    transpose8(dst, lambda c: hT[:, c, b * P:(b + 1) * P]).then_inc(filled, 1)
                elif kind == "wq":
                    m, n = a
                    t = width(m)
                    if n < R_H:
                        dst = open_round(("WQ", m, n))
                        w = tile(step)
                        for h in range(2):
                            for k in range(NC):
                                last = nc.tensor.matmul(dst[:, h, 0:t], w[:, k, h * P:(h + 1) * P], hT[:, k, 0:t],
                                                        start=(k == 0), stop=(k == NC - 1))
                        last.then_inc(filled, 1)
                    if n:
                        dst = open_round(("SC", m, n - 1))
                        wait_drained(pe, ("WQ", m, n - 1))
                        slot, _ = tile_arrival(("wq", m, n - 1))
                        for b in range(len(BLOCKS[m])):
                            for h in range(2):
                                last = nc.tensor.matmul(dst[:, b, h * P:(h + 1) * P], qpT[:, (n - 1) % 2, h, b * P:(b + 1) * P],
                                                        sktiles[:, slot, h, :], start=True, stop=True)
                        last.then_inc(w_used, 1)

        @block.scalar
        def _(act):
            def drain(key, ops):
                for out, src in ops:
                    last = nc.scalar.copy(out, src)
                last.then_inc(drained_by_act, 1)

            def chunks(dst):
                return dst[:, :, :].rearrange("p a (c n) -> p (a c) n", n=P)

            def modulate(key, q, half):
                l, latent = q // 3, int(q % 3 > 0)
                b = place_in_mix(q)
                dst = wait_filled(act, key)
                for part in ((PART_SH1, PART_SC1), (PART_SH2, PART_SC2))[half]:
                    wait_drained(act, ("MC", l, part))
                for c in range(NC):
                    last = nc.scalar.activation(hT[:, c, b * P:(b + 1) * P], chunks(dst)[:, c, :], ACT.Identity,
                                                bias=mod_cols[:, l, 2 * half, c, latent:latent + 1],
                                                scale=mod_cols[:, l, 2 * half + 1, c, latent:latent + 1])
                last.then_inc(drained_by_act, 1)

            def square_root(key):
                n = RMS_HEADS if key[0] == "norm" else 1
                act.wait_ge(root_in_ready, ROOTS[key])
                nc.scalar.activation(root[:, 0:n], root_in[:, 0:n], ACT.Sqrt).then_inc(root_ready, 1)

            def exponentials(q, u):
                nk = 3 * P if MIXES[mix_of(q)][1] else P
                dst = wait_filled(act, ("A", q, u))
                act.wait_ge(neg_max_ready, UNIT[(q, u)])
                for h in range(2):
                    last = nc.scalar.activation(probs[:, u % 2, h, 0:nk], dst[:, h, 0:nk], ACT.Exp,
                                                bias=neg_max[:, u % 2, h:h + 1], scale=SCALE,
                                                accum_out=row_sum[:, u % 2, h:h + 1])
                last.then_inc(drained_by_act, 1)

            def attention(q, u0, u1):
                nk = 3 * P if MIXES[mix_of(q)][1] else P
                exponentials(q, u0)
                for u in range(u0, u1):
                    if u + 1 < u1:
                        exponentials(q, u + 1)
                    dst = wait_filled(act, ("PT", q, u))
                    drain(("PT", q, u), [(pT[:, :, 0:nk], dst[:, :, 0:nk])])

            def expert_weights(q, g0, g1):
                base = q * GROUPS
                with act.Fori(base + g0, base + g1) as g:
                    act.wait_ge(u_used, g * G + 2 * G)
                    nc.scalar.activation(gelu[:, :], dots[:, :], ACT.Gelu).then_inc(gelu_ready, 1)
                    act.wait_ge(weight_ready, g + 1)
                    for j in range(G):
                        act.wait_ge(v_used, g * G + j + 1 + G - DIAGS)
                        nc.scalar.activation(diag[:, j % DIAGS, :], ident, ACT.Copy, scale=weight[:, j:j + 1])\
                            .then_inc(diag_ready, 1)

            act.wait_ge(consts_landed, 16 * N_CONST_DMAS)
            nc.scalar.activation(cond_e[:, :, :], cond[:, :, :], ACT.Exp, scale=-1.0).then_inc(cond_exp, 1)
            for step in SCHEDULE:
                kind, a = step[0], step[1:]
                if kind == "gather":
                    expert_weights(*a)
                elif kind == "xT":
                    modulate(("X", a[0]), a[0], 0)
                elif kind == "proj":
                    m, n = a
                    nb = len(BLOCKS[m])
                    if n == 0 and m:
                        act.wait_ge(route_ready, routes_before(step))
                        if ln_before(step):
                            act.wait_ge(ln_done, ln_before(step))
                        if m == 2:
                            act.wait_ge(kv_stored, 64)
                    dst = wait_filled(act, ("J", m, n))
                    drain(("J", m, n), [(qkv[:, 0:nb, n * TW:(n + 1) * TW], dst[:, 0:nb, 0:TW])])
                elif kind == "norm":
                    q = a[0]
                    wait_drained(act, ("J", mix_of(q), IN_W // TW - 1))
                    if NORM[q] > 1:
                        act.wait_ge(norm_ready, NORM[q] - 1)
                    nc.scalar.activation(squares, qkv[:, place_in_mix(q), G_Q:G_V], ACT.Square).then_inc(squares_ready, 1)
                    square_root(("norm", q))
                elif kind == "qkT":
                    q = a[0]
                    at = slice(place_in_mix(q) * P, (place_in_mix(q) + 1) * P)
                    dst = chunks(wait_filled(act, ("T0", q)))
                    drain(("T0", q), [(qT[:, :, at], dst[:, 0:6, :]), (kT[:, 0:2, at], dst[:, 6:8, :])])
                    dst = chunks(wait_filled(act, ("T1", q)))
                    drain(("T1", q), [(kT[:, 2, at], dst[:, 0, :]), (hT[:, 0:2, at], dst[:, 1:3, :])])
                elif kind == "att":
                    attention(*a)
                elif kind == "four":
                    m = a[0]
                    for b, q in enumerate(BLOCKS[m]):
                        dst = wait_filled(act, ("FY", q))
                        drain(("FY", q), [(fy[:, b, :], dst[:, 0, :])])
                    dst = wait_filled(act, ("FF", m))
                    drain(("FF", m), [(fT[:, :, 0:width(m)], dst[:, :, 0:width(m)])])
                    for b, q in enumerate(BLOCKS[m]):
                        dst = wait_filled(act, ("FO", q))
                        drain(("FO", q), [(qkv[:, b, FN:IN_W], dst[:, 0, 0:IN_W - FN])])
                elif kind == "oT":
                    q = a[0]
                    at = slice(place_in_mix(q) * P, (place_in_mix(q) + 1) * P)
                    dst = wait_filled(act, ("OT", q))
                    drain(("OT", q), [(hT[:, :, at], chunks(dst))])
                elif kind in ("gate", "ln2"):
                    key = ("G", BLOCKS[a[0]][0], 1) if kind == "gate" else ("G", a[0], 2)
                    if ln_before(step):
                        act.wait_ge(ln_done, ln_before(step))
                    if routes_before(step):
                        act.wait_ge(route_ready, routes_before(step))
                    dst = wait_filled(act, key)
                    drain(key, [(gate_b, dst[:, :, :])])
                    if kind == "ln2":
                        square_root(("ln2", a[0]))
                elif kind == "ln1":
                    square_root(("ln1", a[0]))
                elif kind == "h2":
                    q = a[0]
                    modulate(("X2", q), q, 1)
                    if q >= 3:
                        act.wait_ge(ln_done, LN[(q - 3, 2)])
                    dst = wait_filled(act, ("H2", q))
                    drain(("H2", q), [(h_tok[:, q % 3, :].rearrange("p (a n) -> p a n", a=2), dst[:, :, :])])
                elif kind == "wq":
                    m, n = a
                    nb, t = len(BLOCKS[m]), width(m)
                    if n < R_H:
                        dst = wait_filled(act, ("WQ", m, n))
                        drain(("WQ", m, n), [(qpT[:, n % 2, :, 0:t], dst[:, :, 0:t])])
                    if n == 1:
                        act.wait_ge(ln_done, ln_before(step))
                        if not MIXES[m][1]:
                            act.wait_ge(kv_stored, 64 * (MIXES[m][0] + 1))
                    if n:
                        dst = wait_filled(act, ("SC", m, n - 1))
                        drain(("SC", m, n - 1), [(scores[:, 0:nb, (n - 1) * TW:n * TW], dst[:, 0:nb, 0:TW])])
                elif kind == "pick":
                    act.wait_ge(best_ready, ROUTE[a[0]])
                    nc.scalar.activation(gate_e[:, :, :], gate_e[:, :, :], ACT.Exp).then_inc(gate_exp, 1)

        @block.vector
        def _(dve):
            links = [0]

            def link(ins):
                links[0] += 1
                ins.then_inc(dve_chain, 1)
                dve.wait_ge(dve_chain, links[0])

            def spread(ap, shape):
                return ap.to_broadcast(shape)

            def maxima(q, u):
                m, b = mix_of(q), place_in_mix(q)
                nk = 3 * P if MIXES[m][1] else P
                dst = wait_filled(dve, ("A", q, u))
                if MIXES[m][1] and u < 2:
                    link(nc.vector.tensor_tensor(dst[:, :, 0:2 * P], dst[:, :, 0:2 * P], bias[:, b, 2 * u:2 * u + 2, :], ALU.add))
                link(nc.vector.reduce_max(maxes[:, :], dst[:, :, 0:nk], AX.X))
                nc.vector.tensor_scalar(neg_max[:, u % 2, :], maxes[:, :], -SCALE, None, ALU.mult).then_inc(neg_max_ready, 1)
                dve.wait_ge(neg_max_ready, UNIT[(q, u)])

            def attention(q, u0, u1):
                b = place_in_mix(q)
                maxima(q, u0)
                for u in range(u0, u1):
                    if u + 1 < u1:
                        maxima(q, u + 1)
                    wait_drained(dve, ("A", q, u))
                    link(nc.vector.reciprocal(inv_sum[:, :], row_sum[:, u % 2, :]))
                    dst = wait_filled(dve, ("O", q, u))
                    if u < 2:
                        out = qkv[:, b, 2 * u * HD:(2 * u + 2) * HD].rearrange("p (i d) -> p i d", i=2)
                    else:
                        out = qkv[:, b, G_Q:G_Q + Q_H * HD].rearrange("p (g i d) -> p i g d", g=2, i=4)[:, u - 2]
                    nc.vector.tensor_tensor(out, dst[:, 0, 0:2 * HD].rearrange("p (i d) -> p i d", i=2),
                                            spread(inv_sum[:, :].unsqueeze(2), [P, 2, HD]), ALU.mult)\
                        .then_inc(drained_by_dve, 1)
                    wait_drained(dve, ("O", q, u))

            def layer_norm(q, which):
                slot, l = q % 3, q // 3
                x = x_tok[:, slot, :]
                key = (q, which)
                zz = z.rearrange("p (a n) -> p a n", a=2)
                wait_drained(dve, ("G", BLOCKS[mix_of(q)][0] if which == 1 else q, which))
                if which == 1:
                    dst = wait_filled(dve, ("Z", q))
                    if l == 0:
                        dve.wait_ge(x_landed, 48)
                    nc.vector.tensor_tensor(zz, dst[:, :, :], gate_b, ALU.mult).then_inc(drained_by_dve, 1)
                    dve.wait_ge(drained_by_dve, DRAINED_BY_DVE[("Z", q)])
                else:
                    dve.wait_ge(v_used, G + PER_TOKEN * (q + 1))
                    nc.vector.tensor_tensor(zz, acc[:, :, :], gate_b, ALU.mult).then_inc(acc_drained, 1)
                    dve.wait_ge(acc_drained, q + 1)
                link(nc.vector.scalar_tensor_tensor(out=z, in0=x, scalar=ALPHA, in1=z, op0=ALU.mult, op1=ALU.add))
                nc.vector.bn_stats(stats[:, 0, :], z[:, 0:512])
                link(nc.vector.bn_stats(stats[:, 1, :], z[:, 512:D]))
                link(nc.vector.bn_aggr(mean_var[:, :], stats[:, :, :]))
                nc.vector.tensor_scalar(root_in[:, 0:1], mean_var[:, 1:2], LN_EPS, None, ALU.add).then_inc(root_in_ready, 1)
                n = ROOTS[("ln1" if which == 1 else "ln2", q)]
                dve.wait_ge(root_ready, n)
                link(nc.vector.reciprocal(rroot[:, 0:1], root[:, 0:1]))
                link(nc.vector.tensor_scalar(z, z, mean_var[:, 0:1], rroot[:, 0:1], ALU.subtract, ALU.mult))
                dve.wait_ge(ln_rows_landed, 32 * LN[key])
                link(nc.vector.tensor_tensor(z, z, ln_rows[:, 0, :], ALU.mult))
                nc.vector.tensor_tensor(x, z, ln_rows[:, 1, :], ALU.add).then_inc(ln_done, 1)
                dve.wait_ge(ln_done, LN[key])

            def rms_norm_and_rotate(q):
                l, latent, b = q // 3, q % 3 > 0, place_in_mix(q)
                dve.wait_ge(squares_ready, NORM[q])
                link(nc.vector.reduce_sum(root_in[:, :], squares.rearrange("p (h d) -> p h d", d=HD), AX.X))
                nc.vector.tensor_scalar(root_in[:, :], root_in[:, :], 1.0 / HD, RMS_EPS, ALU.mult, ALU.add).then_inc(root_in_ready, 1)
                dve.wait_ge(root_ready, ROOTS[("norm", q)])
                link(nc.vector.reciprocal(rroot[:, :], root[:, :]))
                x = qkv[:, b, G_Q:G_V].rearrange("p (h d) -> p h d", d=HD)
                t1, t2, t3 = (t.rearrange("p (h d) -> p h d", d=HD) for t in (turned, turned2, squares))
                out = [x[:, 0:Q_H].rearrange("p (i g) d -> p g i d", g=KV_H), x[:, Q_H:]]

                def grouped(t):
                    return [t[:, 0:Q_H].rearrange("p (g i) d -> p g i d", g=KV_H), t[:, Q_H:]]

                link(nc.vector.tensor_tensor(t1, x, spread(rroot[:, :].unsqueeze(2), [P, RMS_HEADS, HD]), ALU.mult))
                by = [spread(gains[:, l, 0, :].unsqueeze(1), [P, Q_H, HD]), spread(gains[:, l, 1, :].unsqueeze(1), [P, KV_H, HD])]
                nc.vector.tensor_tensor(t1[:, 0:Q_H], t1[:, 0:Q_H], by[0], ALU.mult)
                link(nc.vector.tensor_tensor(t1[:, Q_H:], t1[:, Q_H:], by[1], ALU.mult))
                if latent:
                    nc.vector.tensor_tensor(t2, t1, spread(rope[:, b, 0, :].unsqueeze(1), [P, RMS_HEADS, HD]), ALU.mult)
                    for half in range(2):
                        for y in range(2):
                            to = slice(32 * half + 16 * y, 32 * half + 16 * y + 16)
                            of = slice(32 * half + 16 * (1 - y), 32 * half + 16 * (1 - y) + 16)
                            last = nc.vector.tensor_tensor(t3[:, :, to], t1[:, :, of],
                                                           spread(rope[:, b, 1, to].unsqueeze(1), [P, RMS_HEADS, 16]), ALU.mult)
                    link(last)
                    for d, s2, s3 in zip(out, grouped(t2), grouped(t3)):
                        last = nc.vector.tensor_tensor(d, s2, s3, ALU.add)
                else:
                    for d, s1 in zip(out, grouped(t1)):
                        last = nc.vector.tensor_copy(d, s1)
                last.then_inc(norm_ready, 1)

            def top_sixteen(groups):
                for v, out, _ in groups:
                    last = nc.vector.max(out=out[:, 0:8], in_=v)
                link(last)
                for v, out, at in groups:
                    last = nc.vector.max_index(out=at[:, 0:8], in_max=out[:, 0:8], in_values=v)
                link(last)
                for v, out, _ in groups:
                    last = nc.vector.match_replace(out=v, in_to_replace=out[:, 0:8], in_values=v, imm_value=LOWEST)
                link(last)
                for v, out, _ in groups:
                    last = nc.vector.max(out=out[:, 8:16], in_=v)
                link(last)
                for v, out, at in groups:
                    last = nc.vector.max_index(out=at[:, 8:16], in_max=out[:, 8:16], in_values=v)
                link(last)

            def pick_experts(q):
                l, slot = q // 3, q % 3
                c4 = cand.rearrange("p (h a b) -> p h a b", h=R_H, a=TOPK)
                top4 = top_s[:, :, :].rearrange("p (h f) k -> p h f k", f=2)
                shape = [P, R_H, TOPK, TOPK]
                link(nc.vector.tensor_tensor(c4, spread(top4[:, :, 0, :].unsqueeze(3), shape),
                                             spread(top4[:, :, 1, :].unsqueeze(2), shape), ALU.add))
                flat = cand.rearrange("p (h n) -> p h n", h=R_H)
                top_sixteen([(flat[:, h], best_s[:, h], best_j[:, h]) for h in range(R_H)])
                nc.vector.tensor_tensor(gate_e[:, :, :], best_s[:, :, :], spread(best_s[:, :, 0:1], [P, R_H, TOPK]), ALU.subtract)\
                    .then_inc(best_ready, 1)
                top_f = scores[:, place_in_mix(q), 0:2 * R_H * TOPK].rearrange("p (h f k) -> p h f k", f=2, k=TOPK)
                link(nc.vector.tensor_copy(top_f, top_i[:, :, :].rearrange("p (h f) k -> p h f k", f=2)))
                j = best_j[:, :, :].rearrange("p h k -> p (h k)")
                hit = cand.rearrange("p (n a) -> p n a", a=TOPK)
                for f, (op, by) in enumerate(((ALU.logical_shift_right, 4), (ALU.bitwise_and, 15))):
                    link(nc.vector.tensor_scalar(half_j[:, :], j, by, None, op))
                    link(nc.vector.tensor_copy(half_f[:, :], half_j[:, :]))
                    link(nc.vector.tensor_tensor(hit, spread(half_f[:, :].unsqueeze(2), [P, PER_TOKEN, TOPK]),
                                                 spread(iota.unsqueeze(1), [P, PER_TOKEN, TOPK]), ALU.is_equal))
                    link(nc.vector.tensor_tensor(c4, c4, spread(top_f[:, :, f, :].unsqueeze(2), shape), ALU.mult))
                    link(nc.vector.reduce_sum(picked[:, f, :], hit, AX.X))
                link(nc.vector.scalar_tensor_tensor(out=picked[:, 0, :], in0=picked[:, 0, :], scalar=float(KEYS),
                                                    in1=picked[:, 1, :], op0=ALU.mult, op1=ALU.add))
                link(nc.vector.tensor_scalar(experts[:, slot, :], picked[:, 0, :], float(l * EXPERTS), None, ALU.add))
                dve.wait_ge(gate_exp, ROUTE[q])
                link(nc.vector.reduce_sum(gate_n[:, :], gate_e[:, :, :], AX.X))
                link(nc.vector.reciprocal(gate_n[:, :], gate_n[:, :]))
                nc.vector.tensor_tensor(gates[:, slot, :].rearrange("p (h k) -> p h k", h=R_H), gate_e[:, :, :],
                                        spread(gate_n[:, :].unsqueeze(2), [P, R_H, TOPK]), ALU.mult).then_inc(route_ready, 1)
                dve.wait_ge(route_ready, ROUTE[q])

            def expert_dots(q, g0, g1):
                slot, base = q % 3, q * GROUPS
                if g0 == 0:
                    wait_drained(dve, ("H2", q))
                    if q == 0:
                        dve.sem_inc(u_used, G)
                with dve.Fori(base + g0, base + g1) as g:
                    for j in range(G):
                        dve.wait_ge(u_used, g * G + j + G)
                        dve.wait_ge(u_landed[j], g * 16 + 16)
                        nc.vector.tensor_tensor_reduce(out=products[:, :], in0=u_rows[:, j, :], in1=h_tok[:, slot, :],
                                                       scale=1.0, scalar=0.0, op0=ALU.mult, op1=ALU.add,
                                                       accum_out=dots[:, j:j + 1]).then_inc(u_used, 1)
                    dve.wait_ge(gelu_ready, g + 1)
                    nc.vector.tensor_tensor(weight[:, :], gelu[:, :], gates[:, slot, bass.ds((g - base) * G, G)], ALU.mult)\
                        .then_inc(weight_ready, 1)

            dve.wait_ge(consts_landed, 16 * N_CONST_DMAS)
            dve.wait_ge(cond_exp, 1)
            link(nc.vector.tensor_scalar(cond_e[:, :, :], cond_e[:, :, :], 1.0, None, ALU.add))
            link(nc.vector.reciprocal(cond_e[:, :, :], cond_e[:, :, :]))
            nc.vector.tensor_tensor(cond_s[:, :, :], cond[:, :, :], cond_e[:, :, :], ALU.mult).then_inc(cond_ready, 1)
            for step in SCHEDULE:
                kind, a = step[0], step[1:]
                if kind == "gather":
                    expert_dots(*a)
                elif kind == "mod":
                    l, c = a
                    gate = c in (PART_G1, PART_G2)
                    at = 32 * l if gate else 64
                    row = mod_rows[at:at + 2, c // PART_G2 if gate else MOD_COLS.index(a) % 2, :]
                    row = row.rearrange("p (a n) -> p a n", a=2)
                    dst = wait_filled(dve, ("MD",) + a)
                    dve.wait_ge(b_landed[(MOD[a] - 1) % 2], 16 * ((MOD[a] + 1) // 2))
                    nc.vector.tensor_tensor(row, dst[at:at + 2, :, :], row, ALU.add).then_inc(drained_by_dve, 1)
                    if not gate:
                        dst = wait_filled(dve, ("MC",) + a)
                        part = (PART_SH1, PART_SC1, PART_SH2, PART_SC2).index(c)
                        nc.vector.tensor_scalar(mod_cols[:, l, part, :, :].rearrange("p c k -> p (c k)"), dst[:, 0, 0:2 * NC],
                                                float(part % 2), None, ALU.add).then_inc(drained_by_dve, 1)
                elif kind == "bias":
                    for half in range(2):
                        dst = wait_filled(dve, ("B", a[0], half))
                        for b in range(2):
                            for r in range(2):
                                part = slice(64 * r, 64 * r + 64)
                                row = 2 * b + r
                                psum = dst[part, :, 0:16 * NA_H * ROW_DIFFS].rearrange("p k (c x) -> p x k c", c=16)
                                mask = window[part, 32 * half:32 * half + 32].rearrange("p (k c) -> p k c", k=2)
                                for h in range(NA_H):
                                    out = bias[part, b, h, :].rearrange("p (j c) -> p j c", j=4)[:, :, 32 * half:32 * half + 32]
                                    at = h * ROW_DIFFS + 3 - row
                                    last = nc.vector.tensor_tensor(out.rearrange("p j (k c) -> p j k c", k=2), psum[:, at:at + 4],
                                                                   spread(mask.unsqueeze(1), [GRID_W, 4, 2, 16]), ALU.add)
                        last.then_inc(drained_by_dve, 1)
                    dve.wait_ge(drained_by_dve, DRAINED_BY_DVE[("B", a[0], 1)])
                elif kind == "norm":
                    rms_norm_and_rotate(a[0])
                elif kind == "att":
                    attention(*a)
                elif kind == "ln1":
                    layer_norm(a[0], 1)
                elif kind == "ln2":
                    layer_norm(a[0], 2)
                elif kind == "top":
                    q, first = a
                    m, b = mix_of(q), place_in_mix(q)
                    wait_drained(dve, ("SC", m, first // 2 + 3))
                    top_sixteen([(scores[:, b, n * KEYS:(n + 1) * KEYS], top_s[:, n], top_i[:, n])
                                 for n in range(first, first + R_H)])
                elif kind == "pick":
                    pick_experts(a[0])


def constants():
    import numpy as np

    def place(name, rows, value):
        a, b = CONST[name]
        out[rows, a:b] = np.asarray(value, np.float64).reshape(out[rows, a:b].shape).astype(np.float32)

    out = np.zeros((P, CONST_W), np.float32)
    place("ident", slice(None), np.eye(P))
    pick = np.zeros((2, 2, P))
    pick[0, 0] = pick[1, 1] = 1.0
    for l in range(DEPTH):
        place("sel", slice(32 * l, 32 * l + 2), pick)
    pos = np.arange(2 * P)
    inv = (1.0 / (np.float32(10000.0) ** (np.arange(16, dtype=np.float32) / np.float32(16)))).astype(np.float32)
    table = np.zeros((2 * P, 2, HD))
    for half, where in enumerate((pos // GRID_W, pos % GRID_W)):
        angle = (where.astype(np.float32)[:, None] * inv).astype(np.float64)
        at = 32 * half
        table[:, 0, at:at + 16] = table[:, 0, at + 16:at + 32] = np.cos(angle)
        table[:, 1, at:at + 16] = -np.sin(angle)
        table[:, 1, at + 16:at + 32] = np.sin(angle)
    place("rope", slice(None), table.reshape(2, P, 2 * HD).transpose(1, 0, 2))

    def dft(n):
        angle = 2 * np.pi * (np.outer(np.arange(n), np.arange(n)) % n) / n
        return np.stack([np.cos(angle), -np.sin(angle)]) / np.sqrt(n)

    place("dft_ctx", slice(None), dft(P).transpose(1, 0, 2))
    place("dft_lat", slice(None), dft(2 * P).reshape(2, 2, P, 2 * P).transpose(2, 1, 0, 3))
    channels = np.zeros((2, HD, 2, 2, HD))
    for g in range(2):
        channels[g, :, 0, g] = dft(HD)[0]
        channels[g, :, 1, g] = -dft(HD)[1]
    place("dft_ch", slice(None), channels.reshape(P, 2 * P))
    col = np.arange(GRID_W)
    start = np.clip(col - 8, 0, GRID_W - 16)
    inside = (col[None] >= start[:, None]) & (col[None] < start[:, None] + 16)
    place("window", slice(None), np.tile(np.where(inside, 0.0, -1e30), (2, 1)))
    shifts = np.zeros((RPB_COLS, 2 * GRID_W))
    shifts[np.arange(RPB_COLS), 78 - np.arange(RPB_COLS)] = 1.0 / SCALE
    place("shift", slice(0, RPB_COLS), shifts)
    place("iota", slice(None), np.tile(np.arange(TOPK), (P, 1)))
    return out


def kernel(**inputs):
    import concourse.bacc as bacc
    import numpy as np
    from concourse.bass_utils import run_bass_kernel_spmd

    a = {k: np.asarray(v) for k, v in inputs.items()}
    n = DEPTH
    wf = np.zeros((2, HD, n, 2, 2, HD), np.float32)
    f = a["w_fourier"].reshape(n, 2, 2, HD, HD)
    for g in range(2):
        wf[g, :, :, :, g] = f[:, :, g].transpose(2, 0, 1, 3)

    def keys_by_channel(k):
        return k.transpose(0, 2, 3, 1).reshape(n, -1, P, P)

    arrays = {
        "x_prompt": a["x_prompt"], "x_sample": a["x_sample"], "consts": constants(),
        "cond": np.stack([a["c_ctx"], a["c"][0]]).reshape(2, NC, P).transpose(2, 1, 0),
        "rpb": a["na_rpb"].transpose(3, 0, 1, 2),
        "gains": np.stack([a["q_gain"], a["k_gain"]], axis=1),
        "wf": wf.reshape(P, n, 2, P),
        "w_mod": a["w_mod"], "b_mod": a["b_mod"], "w_in": a["w_in"], "w_out": a["w_out"], "peer_wq": a["peer_wq"],
        "sub_keys": a["peer_subkeys"].transpose(0, 4, 1, 2, 3).reshape(n, P, 2 * R_H, KEYS),
        "ctx_kT": np.concatenate([keys_by_channel(a["cache_na_k"][0]), keys_by_channel(a["cache_gqa_k"][0])],
                                 axis=1).transpose(0, 2, 1, 3),
        "ctx_v": np.concatenate([a["cache_na_v"][0].reshape(n, P, -1), a["cache_gqa_v"][0].reshape(n, P, -1)], axis=2),
        "ln1_g": a["ln1_g"], "ln1_b": a["ln1_b"], "ln2_g": a["ln2_g"], "ln2_b": a["ln2_b"],
        "peer_u": a["peer_u"].reshape(n * EXPERTS, D), "peer_v": a["peer_v"].reshape(n * EXPERTS, D),
    }
    outs = {"y_prompt": (1, P, D), "y_sample": (1, 2 * P, D), "new_na_k": (n, P, 256), "new_na_v": (n, P, 256),
            "new_gqa_k": (n, P, 128), "new_gqa_v": (n, P, 128)}
    nc = bacc.Bacc("TRN2", target_bir_lowering=False, num_devices=1)
    arrays = {f"in_{k}": np.ascontiguousarray(v) for k, v in arrays.items()}
    i = {k[3:]: nc.dram_tensor(k, v.shape, mybir.dt.from_np(v.dtype), kind="ExternalInput").ap() for k, v in arrays.items()}
    o = {k: nc.dram_tensor(f"out_{k}", s, F32, kind="ExternalOutput").ap() for k, s in outs.items()}
    hybrid_step(nc, i, o)
    got = run_bass_kernel_spmd(nc, [arrays], core_ids=[0]).results[0]
    r = {k: got[f"out_{k}"] for k in outs}
    return (r["y_prompt"], r["y_sample"], r["new_na_k"].reshape(1, n, P, NA_H, HD), r["new_na_v"].reshape(1, n, P, NA_H, HD),
            r["new_gqa_k"].reshape(1, n, P, KV_H, HD), r["new_gqa_v"].reshape(1, n, P, KV_H, HD))
```

```python
from contextlib import ExitStack

import concourse.bass as bass
from concourse import mybir

F32 = mybir.dt.float32
BF16 = mybir.dt.bfloat16
U32 = mybir.dt.uint32
ALU = mybir.AluOpType
ACT = mybir.ActivationFunctionType
AX = mybir.AxisListType

P = 128
DEPTH = 2
D = 1024
NC = D // P
HD = 64
NA_H, Q_H, KV_H = 4, 8, 2
NA_Q, NA_K, NA_V, G_Q = 0, 256, 512, 768
G_K, G_V, FN = 1280, 1408, 1536
IN_W = 1792
RMS_HEADS = Q_H + KV_H
GRID_W = 64
EXPERTS = 16384
R_H, TOPK, KEYS = 8, 16, 128
PER_TOKEN = R_H * TOPK
ALPHA = (2 * DEPTH) ** 0.25
LN_EPS, RMS_EPS = 1e-5, 1e-6
SCALE = HD ** -0.5
LOWEST = -3.0e38

TW = 256
WSLOTS = 3
G = 4
RING = 2 * G
GROUPS = PER_TOKEN // G

MIXES = [(0, 0), (0, 1), (1, 0), (1, 1)]
BLOCKS = [[0], [1, 2], [3], [4, 5]]
PART_SH1, PART_SC1, PART_G1, PART_SH2, PART_SC2, PART_G2 = range(6)


def modulation_steps(l):
    return [("mod", l, c) for c in range(6)]


def mix_steps(m):
    l, latent = MIXES[m]
    qs = BLOCKS[m]
    steps = [("bias", l, 0), ("bias", l, 1)] if latent else []
    steps += [("xT", q) for q in qs]
    steps += [("proj", m, n) for n in range(IN_W // TW)]
    steps += [("norm", q) for q in qs]
    steps += [("qkT", q) for q in qs]
    for q in qs:
        steps += [("att", q, u, u + 2) for u in range(0, 6, 2)]
    steps += [("four", m)]
    steps += [] if latent else [("kvout", qs[0])]
    steps += [("oT", q) for q in qs]
    steps += [("gate", m)]
    steps += [("outp", m, n) for n in range(D // TW)]
    steps += [("ln1", q) for q in qs] + [("h2", q) for q in qs]
    return steps


def query_steps(m):
    return [("wq", m, n) for n in range(R_H + 1)]


def route_steps(q):
    return [("top", q, 0), ("top", q, 8)] + [("pick", q, n) for n in range(4)]


COST = {"mod": 8, "bias": 8, "xT": 5, "proj": 7, "norm": 7, "qkT": 5, "att": 8, "four": 8, "kvout": 0, "oT": 4, "gate": 4,
        "outp": 7, "ln1": 9, "h2": 7, "wq": 8, "top": 10, "pick": 9, "ln2": 10}
TURNS = GROUPS + 1


def beside(q, steps):
    out, at, passed = [], 0, 0
    whole = sum(COST[s[0]] for s in steps)
    for step in steps:
        until = TURNS * passed // max(whole, 1)
        if until > at:
            out.append(("gather", q, at, until))
            at = until
        out.append(step)
        passed += COST[step[0]]
    out.append(("gather", q, at, TURNS))
    return out


def build_schedule():
    mods, first = modulation_steps(0), mix_steps(0)
    gate, ln1 = first.index(("gate", 0)), first.index(("ln1", 0))
    s = mods[:2] + first[:gate] + [mods[2]] + first[gate:ln1 + 1] + mods[3:5] + first[ln1 + 1:]
    s += query_steps(0) + route_steps(0)
    s += beside(0, [mods[5]] + mix_steps(1) + query_steps(1) + route_steps(1))
    ctx = mix_steps(2)
    cut = ctx.index(("att", 3, 0, 2))
    s += beside(1, [("ln2", 0)] + route_steps(2) + modulation_steps(1) + ctx[:cut])
    s += beside(2, [("ln2", 1)] + ctx[cut:] + query_steps(2) + route_steps(3))
    s += beside(3, [("ln2", 2)] + mix_steps(3) + query_steps(3) + route_steps(4))
    s += beside(4, [("ln2", 3)] + route_steps(5))
    s += beside(5, [("ln2", 4)]) + [("ln2", 5)]
    return s


SCHEDULE = build_schedule()


def rounds_of(step):
    kind, a = step[0], step[1:]
    if kind == "mod":
        return [("MD",) + a]
    if kind == "bias":
        return [("B",) + a]
    if kind == "xT":
        return [("X", a[0])]
    if kind == "proj":
        return [("J",) + a]
    if kind == "qkT":
        return [("T0", a[0]), ("T1", a[0])]
    if kind == "att":
        q, u0, u1 = a
        out = [("A", q, u0)]
        for u in range(u0, u1):
            out += ([("A", q, u + 1)] if u + 1 < u1 else []) + [("PT", q, u), ("O", q, u)]
        return out
    if kind == "four":
        qs = BLOCKS[a[0]]
        return [("FY", q) for q in qs] + [("FF", a[0])] + [("FO", q) for q in qs]
    if kind == "oT":
        return [("OT", a[0])]
    if kind == "gate":
        return [("G", BLOCKS[a[0]][0], 1)]
    if kind == "outp":
        return [("Z", q) for q in BLOCKS[a[0]]] if a[1] == 0 else []
    if kind == "h2":
        return [("X2", a[0]), ("H2", a[0])]
    if kind == "wq":
        m, n = a
        return ([("WQ", m, n)] if n < R_H else []) + ([("SC", m, n - 1)] if n else [])
    if kind == "ln2":
        return [("G", a[0], 2)]
    return []


ROUNDS = [r for s in SCHEDULE for r in rounds_of(s)]
PAIRS = 3
ROUND = {r: n for n, r in enumerate(ROUNDS)}
BY_DVE = {"MD", "B", "O", "Z"}
BY_TILE = {"MD", "J", "Z", "SC"}


def numbered(kinds, keys):
    return {k: n + 1 for n, k in enumerate(k for s in SCHEDULE if s[0] in kinds for k in keys(s))}


def counted(rounds):
    return {r: n + 1 for n, r in enumerate(rounds)}


DRAINED_BY_DVE = counted(r for r in ROUNDS if r[0] in BY_DVE)
DRAINED_BY_ACT = counted(r for r in ROUNDS if r[0] not in BY_DVE)
FILLED = counted(r for r in ROUNDS if r[0] not in BY_TILE)
LN = numbered(("ln1", "ln2"), lambda s: [(s[1], 1 if s[0] == "ln1" else 2)])
NORM = numbered(("norm",), lambda s: [s[1]])
ROOTS = numbered(("norm", "ln1", "ln2"), lambda s: [(s[0], s[1])])
UNIT = numbered(("att",), lambda s: [(s[1], u) for u in range(s[2], s[3])])
ROUTE = numbered(("pick",), lambda s: [s[1]] if s[2] == 3 else [])
GATE = numbered(("gate", "ln2"), lambda s: [(BLOCKS[s[1]][0], 1) if s[0] == "gate" else (s[1], 2)])
TILES = numbered(("mod", "proj", "outp", "wq"),
                 lambda s: [s + (t,) for t in range(4)] if s[0] == "mod" else [] if s[0] == "wq" and s[2] == R_H else [s])


def ln_before(step):
    return sum(s[0] in ("ln1", "ln2") for s in SCHEDULE[:SCHEDULE.index(step)])


def routes_before(step):
    return sum(s[0] == "pick" and s[2] == 3 for s in SCHEDULE[:SCHEDULE.index(step)])


def mix_of(q):
    return next(m for m in range(4) if q in BLOCKS[m])


def place_in_mix(q):
    return q - BLOCKS[mix_of(q)][0]


def width(m):
    return P * len(BLOCKS[m])


def last_tile(key):
    kind = key[0]
    if kind == "MD":
        return ("mod",) + key[1:] + (3,)
    if kind == "Z":
        return ("outp", mix_of(key[1]), 3)
    return ({"J": "proj", "SC": "wq"}[kind],) + key[1:]


def tile_arrival(key):
    n = TILES[key]
    slot = (n - 1) % WSLOTS
    return slot, 16 * sum(2 if k[0] == "wq" else 1 for k, v in TILES.items() if (v - 1) % WSLOTS == slot and v <= n)


CONST = {}
_at = 0
for _name, _n in (("ident", P), ("ones", P), ("rope", 2 * 2 * HD), ("dft_ctx", 2 * P), ("dft_lat", 2 * 2 * 2 * P),
                  ("dft_ch", 2 * P), ("window", GRID_W), ("shift", 2 * GRID_W), ("iota", TOPK), ("zero", P)):
    CONST[_name] = (_at, _at + _n)
    _at += _n
CONST_W = _at
RPB_ROWS, RPB_COLS = 15, 31
ROW_DIFFS = 7


def hybrid_step(nc, i, o):
    ctx = ExitStack()
    with ctx:
        def sb(name, shape, dt=F32):
            return ctx.enter_context(nc.sbuf_tensor(name, shape, dt))

        def sem(name):
            return ctx.enter_context(nc.semaphore(name))

        u_rows = sb("u_rows", [P, RING, D])
        v_rows = sb("v_rows", [P, RING, D])
        wtiles = sb("wtiles", [P, WSLOTS, NC, TW])
        sktiles = sb("sktiles", [P, WSLOTS, 2, KEYS])
        x_tok = sb("x_tok", [P, 3, D])
        h_tok = sb("h_tok", [P, 3, D])
        hT = sb("hT", [P, NC, 2 * P])
        mod_cols = sb("mod_cols", [P, DEPTH, 6, NC, 2])
        b_mod = sb("b_mod_cols", [P, DEPTH, 6, NC])
        rows = sb("rows", [P, 2 * D])
        ln_rows = rows[:, :].rearrange("p (r n) -> p r n", r=2)
        bias = rows[:, :].rearrange("p (b h n) -> p b h n", b=2, h=NA_H)
        arena = sb("arena", [P, 7424])
        qT = sb("qT", [P, 6, 2 * P])
        kT = sb("kT", [P, 3, 3 * P])
        consts = sb("consts", [P, CONST_W])
        rpb = sb("rpb", [RPB_COLS, DEPTH, NA_H, RPB_ROWS])
        gains = sb("gains", [P, DEPTH, 2, HD])
        wf = sb("wf", [P, DEPTH, 2, P])
        v_ctx = sb("v_ctx", [P, (NA_H + KV_H) * HD])
        cond = sb("cond", [P, NC, 2])
        cond_e = sb("cond_e", [P, NC, 2])
        cond_s = sb("cond_s", [P, NC, 2])
        stats = sb("stats", [P, 2, 6])
        mean_var = sb("mean_var", [P, 2])
        root_in = sb("root_in", [P, RMS_HEADS])
        root = sb("root", [P, RMS_HEADS])
        rroot = sb("rroot", [P, RMS_HEADS])
        maxes = sb("maxes", [P, 2])
        neg_max = sb("neg_max", [P, 2, 2])
        row_sum = sb("row_sum", [P, 2, 2])
        inv_sum = sb("inv_sum", [P, 2])
        top_s = sb("top_s", [P, 2 * R_H, TOPK])
        top_i = sb("top_i", [P, 2 * R_H, TOPK], U32)
        best_s = sb("best_s", [P, R_H, TOPK])
        best_j = sb("best_j", [P, R_H, TOPK], U32)
        half_j = sb("half_j", [P, PER_TOKEN], U32)
        half_f = sb("half_f", [P, PER_TOKEN])
        picked = sb("picked", [P, 2, PER_TOKEN])
        gate_e = sb("gate_e", [P, R_H, TOPK])
        gate_n = sb("gate_n", [P, R_H])
        experts = sb("experts", [P, 3, PER_TOKEN], U32)
        gates = sb("gates", [P, 3, PER_TOKEN])
        products = sb("products", [P, D], BF16)
        u_index = sb("u_index", [P, 2, RING], U32)
        v_index = sb("v_index", [P, 2, RING], U32)
        dots = sb("dots", [P, 2, G])
        gelu = sb("gelu", [P, 2, G])
        weight = sb("weight", [P, 2, G])
        diag = sb("diag", [P, 2, G, P])
        qkv = arena[:, 0:2 * IN_W].rearrange("p (b n) -> p b n", b=2)
        probs = arena[:, 3584:5120].rearrange("p (a i n) -> p a i n", a=2, i=2)
        pT = arena[:, 5120:5888].rearrange("p (i n) -> p i n", i=2)
        fy = arena[:, 5888:6912].rearrange("p (b n) -> p b n", b=2)
        fT = arena[:, 6912:7424].rearrange("p (g n) -> p g n", g=2)
        squares = arena[:, 3584:3584 + RMS_HEADS * HD]
        turned = arena[:, 3584 + 640:3584 + 1280]
        turned2 = arena[:, 3584 + 1280:3584 + 1920]
        gate_b = arena[:, 5120:5120 + D].rearrange("p (a n) -> p a n", a=2)
        z = arena[:, 6144:6144 + D]
        scores = arena[:, 0:2 * 2048].rearrange("p (b n) -> p b n", b=2)
        cand = arena[:, 4096:6144]
        qpT = arena[:, 6144:6144 + 1024].rearrange("p (a i n) -> p a i n", a=2, i=2)

        def const(name):
            a, b = CONST[name]
            return consts[:, a:b]

        ident = const("ident")
        ones = const("ones")
        rope = const("rope").rearrange("p (b f n) -> p b f n", b=2, f=2)
        dft_ctx = const("dft_ctx").rearrange("p (f n) -> p f n", f=2)
        dft_lat = const("dft_lat").rearrange("p (b f n) -> p b f n", b=2, f=2)
        dft_ch = const("dft_ch")
        window = const("window")
        shift = const("shift")
        iota = const("iota")

        acc = ctx.enter_context(nc.psum_tensor("acc", [P, 2, 512], F32))
        pairs = [ctx.enter_context(nc.psum_tensor(f"pair{n}", [P, 2, 512], F32)) for n in range(PAIRS)]

        consts_landed = sem("consts_landed")
        x_landed = sem("x_landed")
        w_landed = [sem(f"w_landed{n}") for n in range(WSLOTS)]
        w_used = sem("w_used")
        gate_diag_ready = sem("gate_diag_ready")
        ln_rows_landed = sem("ln_rows_landed")
        ctx_landed = sem("ctx_landed")
        kv_stored = sem("kv_stored")
        y_stored = sem("y_stored")
        filled = sem("filled")
        drained_by_act = sem("drained_by_act")
        drained_by_dve = sem("drained_by_dve")
        cond_exp = sem("cond_exp")
        cond_ready = sem("cond_ready")
        squares_ready = sem("squares_ready")
        root_in_ready = sem("root_in_ready")
        root_ready = sem("root_ready")
        norm_ready = sem("norm_ready")
        neg_max_ready = sem("neg_max_ready")
        ln_done = sem("ln_done")
        best_ready = sem("best_ready")
        gate_exp = sem("gate_exp")
        route_ready = sem("route_ready")
        acc_drained = sem("acc_drained")
        index_copied = sem("index_copied")
        issue_granted = sem("issue_granted")
        u_landed = [sem(f"u_landed{n}") for n in range(RING)]
        v_landed = [sem(f"v_landed{n}") for n in range(RING)]
        u_used = sem("u_used")
        v_used = sem("v_used")
        gelu_ready = sem("gelu_ready")
        weight_ready = sem("weight_ready")
        diag_ready = sem("diag_ready")
        dve_chain = sem("dve_chain")
        act_chain = sem("act_chain")

        N_CONST_DMAS = 6

        def pair(key):
            return pairs[ROUND[key] % PAIRS]

        def wait_filled(eng, key):
            if key[0] in BY_TILE:
                eng.wait_ge(w_used, TILES[last_tile(key)])
            else:
                eng.wait_ge(filled, FILLED[key])
            return pair(key)

        def wait_drained(eng, key):
            if key[0] in BY_DVE:
                eng.wait_ge(drained_by_dve, DRAINED_BY_DVE[key])
            else:
                eng.wait_ge(drained_by_act, DRAINED_BY_ACT[key])

        def turns_of(eng, q, h0, h1, turn, before=False):
            base = q * GROUPS

            def one(h):
                n = base + h - before
                turn(n // 2, n % 2)

            if h0 < h1 and (h0 - before) % 2:
                one(h0)
                h0 += 1
            if h1 - h0 >= 2:
                start = (base + h0 - before) // 2
                with eng.Fori(start, start + (h1 - h0) // 2) as p:
                    turn(p, 0)
                    turn(p, 1)
                h0 += (h1 - h0) // 2 * 2
            if h0 < h1:
                one(h0)

        block = ctx.enter_context(nc.Block())

        @block.sync
        def _(sp):
            sp.dma_start(consts[:, :], i["consts"]).then_inc(consts_landed, 16)
            sp.dma_start(cond[:, :, :], i["cond"]).then_inc(consts_landed, 16)
            for b, src in enumerate((i["x_prompt"][0], i["x_sample"][0, 0:P], i["x_sample"][0, P:2 * P])):
                sp.dma_start(x_tok[:, b, :], src).then_inc(x_landed, 16)
            sp.dma_start(rpb[:, :, :, :], i["rpb"]).then_inc(consts_landed, 16)
            sp.dma_start(gains[:, :, :, :], i["gains"].partition_broadcast(P)).then_inc(consts_landed, 16)
            sp.dma_start(wf[:, :, :, :], i["wf"]).then_inc(consts_landed, 16)
            sp.dma_start(b_mod[:, :, :, :], i["b_mod"]).then_inc(consts_landed, 16)

            def weights(key, src):
                n = TILES[key]
                slot = (n - 1) % WSLOTS
                if n > WSLOTS:
                    sp.wait_ge(w_used, n - WSLOTS)
                sp.dma_start(wtiles[:, slot, :, :], src).then_inc(w_landed[slot], 16)
                return slot

            def cols(w, l, n):
                return w[l, :, n * TW:(n + 1) * TW].rearrange("(c p) n -> p c n", p=P)

            for step in SCHEDULE:
                kind, a = step[0], step[1:]
                if kind == "mod":
                    l, c = a
                    for t in range(4):
                        weights(step + (t,), cols(i["w_mod"], l, 4 * c + t))
                elif kind == "proj":
                    weights(step, cols(i["w_in"], MIXES[a[0]][0], a[1]))
                elif kind == "outp":
                    weights(step, cols(i["w_out"], MIXES[a[0]][0], a[1]))
                elif kind == "wq" and a[1] < R_H:
                    l = MIXES[a[0]][0]
                    slot = weights(step, cols(i["peer_wq"], l, a[1]))
                    sp.dma_start(sktiles[:, slot, :, :], i["sub_keys"][l, :, 2 * a[1]:2 * a[1] + 2, :])\
                        .then_inc(w_landed[slot], 16)
                elif kind == "bias" and a[1] == 0:
                    l = a[0]
                    if l:
                        wait_filled(sp, ("O", 2, 5))
                    sp.dma_start(kT[:, :, 2 * P:3 * P], i["ctx_kT"][l]).then_inc(ctx_landed, 16)
                    sp.dma_start(v_ctx[:, :], i["ctx_v"][l]).then_inc(ctx_landed, 16)
                elif kind in ("ln1", "ln2"):
                    which = 1 if kind == "ln1" else 2
                    n, l = LN[(a[0], which)], a[0] // 3
                    if n > 1:
                        sp.wait_ge(ln_done, n - 1)
                    if which == 1 and MIXES[mix_of(a[0])][1]:
                        wait_filled(sp, ("O", BLOCKS[mix_of(a[0])][-1], 5))
                    for r, name in enumerate((f"ln{which}_g", f"ln{which}_b")):
                        sp.dma_start(ln_rows[:, r, :], i[name][l, :].partition_broadcast(P))\
                            .then_inc(ln_rows_landed, 16)
                    if kind == "ln2" and l == DEPTH - 1:
                        sp.wait_ge(ln_done, n)
                        dst = o["y_prompt"][0] if a[0] == 3 else o["y_sample"][0, (a[0] - 4) * P:(a[0] - 3) * P]
                        sp.dma_start(dst, x_tok[:, a[0] % 3, :]).then_inc(y_stored, 16)
                elif kind == "kvout":
                    q = a[0]
                    l = q // 3
                    sp.wait_ge(norm_ready, NORM[q])
                    for name, at, n in (("new_na_k", NA_K, 256), ("new_na_v", NA_V, 256),
                                        ("new_gqa_k", G_K, 128), ("new_gqa_v", G_V, 128)):
                        sp.dma_start(o[name][l], qkv[:, 0, at:at + n]).then_inc(kv_stored, 16)
            sp.wait_ge(kv_stored, 16 * 8)
            sp.wait_ge(y_stored, 16 * 3)

        @block.gpsimd
        def _(pool):
            def gather_u(turn, slot, half):
                pool.wait_ge(u_used, turn * RING + slot + 1)
                pool.sem_inc(issue_granted, 1)
                pool.indirect_dma_start(
                    out=u_rows[:, slot, :], out_offset=None, in_=i["peer_u"],
                    in_offset=bass.IndirectOffsetOnAxis(ap=u_index[:, half, slot:slot + 1], axis=0),
                ).then_inc(u_landed[slot], 16)

            def gather_v(turn, slot, half):
                pool.wait_ge(v_used, turn * RING + slot + 1)
                pool.sem_inc(issue_granted, 1)
                at = (slot + G) % RING
                pool.indirect_dma_start(
                    out=v_rows[:, slot, :], out_offset=None, in_=i["peer_v"],
                    in_offset=bass.IndirectOffsetOnAxis(ap=v_index[:, half, at:at + 1], axis=0),
                ).then_inc(v_landed[slot], 16)

            RINGS = PER_TOKEN // RING

            def phase(q, n, half):
                first, last = type(n) is int and n == 0, type(n) is int and n == RINGS
                e = experts[:, q % 3, :]
                if not last:
                    pool.tensor_copy(u_index[:, half, :], e[:, bass.ds(n * RING, RING)]).then_inc(index_copied, 1)
                if first:
                    pool.tensor_copy(v_index[:, half, G:], e[:, 0:G]).then_inc(index_copied, 1)
                elif last:
                    pool.tensor_copy(v_index[:, half, 0:G], e[:, PER_TOKEN - G:]).then_inc(index_copied, 1)
                else:
                    pool.tensor_copy(v_index[:, half, :], e[:, bass.ds(n * RING - G, RING)]).then_inc(index_copied, 1)
                pool.wait_ge(index_copied, q * (2 * RINGS + 1) + n * 2 + (1 if last else 2))
                for j in range(RING):
                    if not last:
                        gather_u(n + q * RINGS, j, half)
                    if j < G and not first:
                        gather_v(n + q * RINGS - 1, j + G, half)
                    if j >= G and not last:
                        gather_v(n + q * RINGS, j - G, half)

            for q in range(6):
                pool.wait_ge(route_ready, ROUTE[q])
                phase(q, 0, 0)
                with pool.Fori(1, RINGS - 1, 2) as n:
                    phase(q, n, 1)
                    phase(q, n + 1, 0)
                phase(q, RINGS - 1, 1)
                phase(q, RINGS, 0)

        @block.tensor
        def _(pe):
            def open_round(key):
                if ROUND[key] >= PAIRS:
                    wait_drained(pe, ROUNDS[ROUND[key] - PAIRS])
                return pair(key)

            def tile(key):
                slot, n = tile_arrival(key)
                pe.wait_ge(w_landed[slot], n)
                return wtiles[:, slot, :, :]

            def transpose8(dst, src):
                for c in range(NC):
                    last = nc.tensor.transpose(dst[:, c // 4, (c % 4) * P:(c % 4 + 1) * P], src(c), ident)
                return last

            def scores_round(q, u):
                m, b = mix_of(q), place_in_mix(q)
                nk = 3 * P if MIXES[m][1] else P
                dst = open_round(("A", q, u))
                kp = min(u, 2)
                for h in range(2):
                    rows = slice(64 * h, 64 * h + 64)
                    last = nc.tensor.matmul(dst[:, h, 0:nk], qT[rows, u, b * P:(b + 1) * P], kT[rows, kp, 0:nk],
                                            start=True, stop=True)
                last.then_inc(filled, 1)

            def attention(q, u0, u1):
                m = mix_of(q)
                b, latent = place_in_mix(q), MIXES[m][1]
                chunks = 3 if latent else 1
                wait_drained(pe, ("T1", BLOCKS[m][-1]))
                if latent:
                    pe.wait_ge(ctx_landed, 32 * (q // 3 + 1))
                scores_round(q, u0)
                for u in range(u0, u1):
                    if u + 1 < u1:
                        scores_round(q, u + 1)
                    dst = open_round(("PT", q, u))
                    wait_drained(pe, ("A", q, u))
                    for h in range(2):
                        for k in range(chunks):
                            last = nc.tensor.transpose(dst[:, h, k * P:(k + 1) * P], probs[:, u % 2, h, k * P:(k + 1) * P], ident)
                    last.then_inc(filled, 1)
                    dst = open_round(("O", q, u))
                    wait_drained(pe, ("PT", q, u))
                    for h in range(2):
                        own = (NA_V + (2 * u + h) * HD) if u < 2 else (G_V + h * HD)
                        old = ((2 * u + h) * HD) if u < 2 else (256 + h * HD)
                        for k in range(chunks):
                            v = v_ctx[:, old:old + HD] if k == 2 else qkv[:, k, own:own + HD]
                            last = nc.tensor.matmul(dst[:, 0, h * HD:(h + 1) * HD], pT[:, h, k * P:(k + 1) * P], v,
                                                    start=(k == 0), stop=(k == chunks - 1))
                    last.then_inc(filled, 1)

            def fourier(m):
                l, latent = MIXES[m]
                qs = BLOCKS[m]
                t = width(m)
                for b, q in enumerate(qs):
                    dst = open_round(("FY", q))
                    for g in range(2):
                        last = nc.tensor.matmul(dst[:, 0, g * 256:(g + 1) * 256], hT[:, g, b * P:(b + 1) * P], dft_ch,
                                                start=True, stop=True)
                    last.then_inc(filled, 1)
                dst = open_round(("FF", m))
                wait_drained(pe, ("FY", qs[-1]))
                for g in range(2):
                    for b in range(len(qs)):
                        for f in range(2):
                            table = dft_lat[:, b, f, :] if latent else dft_ctx[:, f, :]
                            last = nc.tensor.matmul(dst[:, g, 0:t], fy[:, b, g * 256 + f * P:g * 256 + (f + 1) * P], table,
                                                    start=(b == 0 and f == 0), stop=(b == len(qs) - 1 and f == 1))
                last.then_inc(filled, 1)
                for b, q in enumerate(qs):
                    dst = open_round(("FO", q))
                    wait_drained(pe, ("FF", m))
                    for g in range(2):
                        last = nc.tensor.matmul(dst[:, 0, g * P:(g + 1) * P], fT[:, g, b * P:(b + 1) * P], wf[:, l, g, :],
                                                start=True, stop=True)
                    last.then_inc(filled, 1)

            def experts_sum(q, h0, h1):
                if h0 == 0 and q == 0:
                    pe.sem_inc(v_used, RING)

                def turn(pairs_before, half):
                    for j in range(G):
                        slot = half * G + j
                        pe.wait_ge(diag_ready, pairs_before * RING + slot + 1)
                        pe.wait_ge(v_landed[slot], pairs_before * 16 + 16)
                        for n in range(2):
                            last = nc.tensor.matmul(acc[:, n, :], diag[:, half, j, :], v_rows[:, slot, n * 512:(n + 1) * 512],
                                                    start=False, stop=True, skip_group_check=True)
                        last.then_inc(v_used, 1)

                if h0 <= 1 < h1:
                    if q:
                        pe.wait_ge(acc_drained, q)
                    for n in range(2):
                        nc.tensor.matmul(acc[:, n, :], const("zero")[0:1, :], consts[0:1, 0:512], start=True, stop=True)
                turns_of(pe, q, max(h0, 1), h1, lambda p, half: turn(p, half), before=True)

            pe.wait_ge(consts_landed, 16 * N_CONST_DMAS)
            for step in SCHEDULE:
                kind, a = step[0], step[1:]
                if kind == "gather":
                    experts_sum(*a)
                elif kind == "mod":
                    l, c = a
                    dst = open_round(("MD",) + a)
                    pe.wait_ge(cond_ready, 1)
                    for t in range(4):
                        w = tile(step + (t,))
                        for n in range(2):
                            for k in range(NC):
                                last = nc.tensor.matmul(dst[:, 0, 4 * t + 2 * n:4 * t + 2 * n + 2], w[:, k, n * P:(n + 1) * P],
                                                        cond_s[:, k, :], start=(k == 0), stop=(k == NC - 1))
                        last.then_inc(w_used, 1)
                elif kind == "bias":
                    l, half = a
                    dst = open_round(("B", l, half))
                    for c in range(32):
                        key_col = 32 * half + c
                        pick = shift[0:RPB_COLS, 63 - key_col:127 - key_col]
                        at = (c % 16) * NA_H * ROW_DIFFS
                        for row in range(2):
                            out = dst[64 * row:64 * row + 64, c // 16, at:at + NA_H * ROW_DIFFS]
                            last = nc.tensor.matmul(out.rearrange("p (h r) -> p h r", h=NA_H), pick,
                                                    rpb[:, l, :, 4:4 + ROW_DIFFS], start=True, stop=True)
                    last.then_inc(filled, 1)
                elif kind == "xT":
                    q = a[0]
                    dst = open_round(("X", q))
                    if q < 3:
                        pe.wait_ge(x_landed, 48)
                    else:
                        pe.wait_ge(ln_done, LN[(q - 3, 2)])
                    transpose8(dst, lambda c: x_tok[:, q % 3, c * P:(c + 1) * P]).then_inc(filled, 1)
                elif kind in ("proj", "outp"):
                    m, n = a
                    w = tile(step)
                    if n == 0:
                        for q in BLOCKS[m]:
                            wait_drained(pe, ("X" if kind == "proj" else "OT", q))
                    if kind == "proj":
                        both = open_round(("J", m, n))
                    for b, q in enumerate(BLOCKS[m]):
                        if kind == "outp":
                            dst = open_round(("Z", q)) if n == 0 else pair(("Z", q))
                            dst = dst[:, n // 2, (n % 2) * TW:(n % 2 + 1) * TW]
                        else:
                            dst = both[:, b, 0:TW]
                        for k in range(NC):
                            last = nc.tensor.matmul(dst, hT[:, k, b * P:(b + 1) * P], w[:, k, :],
                                                    start=(k == 0), stop=(k == NC - 1))
                    last.then_inc(w_used, 1)
                elif kind == "qkT":
                    q = a[0]
                    b = place_in_mix(q)
                    src = qkv[:, b, :]
                    dst = open_round(("T0", q))
                    pe.wait_ge(norm_ready, NORM[q])
                    wait_drained(pe, ("J", mix_of(q), IN_W // TW - 1))
                    parts = [src[:, NA_Q + k * P:NA_Q + (k + 1) * P] for k in range(2)]
                    parts += [src[:, G_Q + k * P:G_Q + (k + 1) * P] for k in range(4)]
                    parts += [src[:, NA_K + k * P:NA_K + (k + 1) * P] for k in range(2)]
                    transpose8(dst, lambda c: parts[c]).then_inc(filled, 1)
                    dst = open_round(("T1", q))
                    for k, at in enumerate((G_K, FN, FN + P)):
                        last = nc.tensor.transpose(dst[:, 0, k * P:(k + 1) * P], src[:, at:at + P], ident)
                    last.then_inc(filled, 1)
                elif kind == "att":
                    attention(*a)
                elif kind == "four":
                    fourier(a[0])
                elif kind == "oT":
                    q = a[0]
                    b = place_in_mix(q)
                    dst = open_round(("OT", q))
                    wait_drained(pe, ("O", q, 5))
                    wait_drained(pe, ("FO", q))
                    at = [NA_Q, NA_Q + P, G_Q, G_Q + P, G_Q + 2 * P, G_Q + 3 * P, FN, FN + P]
                    transpose8(dst, lambda c: qkv[:, b, at[c]:at[c] + P]).then_inc(filled, 1)
                elif kind in ("gate", "ln2"):
                    q, which = (BLOCKS[a[0]][0], 1) if kind == "gate" else (a[0], 2)
                    dst = open_round(("G", q, which))
                    pe.wait_ge(gate_diag_ready, GATE[(q, which)])
                    for n in range(2):
                        last = nc.tensor.matmul(dst[:, n, :], ones, z[:, n * 512:(n + 1) * 512], start=True, stop=True)
                    last.then_inc(filled, 1)
                elif kind == "h2":
                    q = a[0]
                    b = place_in_mix(q)
                    dst = open_round(("X2", q))
                    pe.wait_ge(ln_done, LN[(q, 1)])
                    transpose8(dst, lambda c: x_tok[:, q % 3, c * P:(c + 1) * P]).then_inc(filled, 1)
                    dst = open_round(("H2", q))
                    wait_drained(pe, ("X2", q))
                    transpose8(dst, lambda c: hT[:, c, b * P:(b + 1) * P]).then_inc(filled, 1)
                elif kind == "wq":
                    m, n = a
                    t = width(m)
                    if n < R_H:
                        dst = open_round(("WQ", m, n))
                        w = tile(step)
                        for h in range(2):
                            for k in range(NC):
                                last = nc.tensor.matmul(dst[:, h, 0:t], w[:, k, h * P:(h + 1) * P], hT[:, k, 0:t],
                                                        start=(k == 0), stop=(k == NC - 1))
                        last.then_inc(filled, 1)
                    if n:
                        dst = open_round(("SC", m, n - 1))
                        wait_drained(pe, ("WQ", m, n - 1))
                        slot, _ = tile_arrival(("wq", m, n - 1))
                        for b in range(len(BLOCKS[m])):
                            for h in range(2):
                                last = nc.tensor.matmul(dst[:, b, h * P:(h + 1) * P], qpT[:, (n - 1) % 2, h, b * P:(b + 1) * P],
                                                        sktiles[:, slot, h, :], start=True, stop=True)
                        last.then_inc(w_used, 1)

        @block.scalar
        def _(act):
            def drain(key, ops):
                for out, src in ops:
                    last = nc.scalar.copy(out, src)
                last.then_inc(drained_by_act, 1)

            def chunks(dst):
                return dst[:, :, :].rearrange("p a (c n) -> p (a c) n", n=P)

            def modulate(key, q, half):
                l, latent = q // 3, int(q % 3 > 0)
                b = place_in_mix(q)
                dst = wait_filled(act, key)
                for part in ((PART_SH1, PART_SC1), (PART_SH2, PART_SC2))[half]:
                    wait_drained(act, ("MD", l, part))
                for c in range(NC):
                    last = nc.scalar.activation(hT[:, c, b * P:(b + 1) * P], chunks(dst)[:, c, :], ACT.Identity,
                                                bias=mod_cols[:, l, 3 * half, c, latent:latent + 1],
                                                scale=mod_cols[:, l, 3 * half + 1, c, latent:latent + 1])
                last.then_inc(drained_by_act, 1)

            def square_root(key):
                n = RMS_HEADS if key[0] == "norm" else 1
                act.wait_ge(root_in_ready, ROOTS[key])
                nc.scalar.activation(root[:, 0:n], root_in[:, 0:n], ACT.Sqrt).then_inc(root_ready, 1)

            def exponentials(q, u):
                nk = 3 * P if MIXES[mix_of(q)][1] else P
                dst = wait_filled(act, ("A", q, u))
                act.wait_ge(neg_max_ready, UNIT[(q, u)])
                for h in range(2):
                    last = nc.scalar.activation(probs[:, u % 2, h, 0:nk], dst[:, h, 0:nk], ACT.Exp,
                                                bias=neg_max[:, u % 2, h:h + 1], scale=SCALE,
                                                accum_out=row_sum[:, u % 2, h:h + 1])
                last.then_inc(drained_by_act, 1)

            def attention(q, u0, u1):
                nk = 3 * P if MIXES[mix_of(q)][1] else P
                exponentials(q, u0)
                for u in range(u0, u1):
                    if u + 1 < u1:
                        exponentials(q, u + 1)
                    dst = wait_filled(act, ("PT", q, u))
                    drain(("PT", q, u), [(pT[:, :, 0:nk], dst[:, :, 0:nk])])

            def expert_weights(q, h0, h1):
                def diagonals(p, half):
                    act.wait_ge(weight_ready, p * 2 + half + 1)
                    for j in range(G):
                        act.wait_ge(v_used, p * RING + half * G + j + 1)
                        nc.scalar.activation(diag[:, half, j, :], ident, ACT.Copy, scale=weight[:, half, j:j + 1])\
                            .then_inc(diag_ready, 1)

                def gelus(p, half):
                    act.wait_ge(u_used, p * RING + (half + 1) * G + RING)
                    nc.scalar.activation(gelu[:, half, :], dots[:, half, :], ACT.Gelu).then_inc(gelu_ready, 1)

                def turn(p, half):
                    diagonals(p - 1 if half == 0 else p, 1 - half)
                    gelus(p, half)

                base = q * GROUPS
                if h0 == 0:
                    gelus(base // 2, 0)
                turns_of(act, q, max(h0, 1), min(h1, GROUPS), turn)
                if h1 == TURNS:
                    diagonals((base + GROUPS - 1) // 2, 1)

            act.wait_ge(consts_landed, 16 * N_CONST_DMAS)
            nc.scalar.activation(cond_e[:, :, :], cond[:, :, :], ACT.Exp, scale=-1.0).then_inc(cond_exp, 1)
            for step in SCHEDULE:
                kind, a = step[0], step[1:]
                if kind == "gather":
                    expert_weights(*a)
                elif kind == "xT":
                    modulate(("X", a[0]), a[0], 0)
                elif kind == "proj":
                    m, n = a
                    nb = len(BLOCKS[m])
                    if n == 0 and m:
                        act.wait_ge(route_ready, routes_before(step))
                        if ln_before(step):
                            act.wait_ge(ln_done, ln_before(step))
                        if m == 2:
                            act.wait_ge(kv_stored, 64)
                    dst = wait_filled(act, ("J", m, n))
                    drain(("J", m, n), [(qkv[:, 0:nb, n * TW:(n + 1) * TW], dst[:, 0:nb, 0:TW])])
                elif kind == "norm":
                    q = a[0]
                    wait_drained(act, ("J", mix_of(q), IN_W // TW - 1))
                    if NORM[q] > 1:
                        act.wait_ge(norm_ready, NORM[q] - 1)
                    nc.scalar.activation(squares, qkv[:, place_in_mix(q), G_Q:G_V], ACT.Square).then_inc(squares_ready, 1)
                    square_root(("norm", q))
                elif kind == "qkT":
                    q = a[0]
                    at = slice(place_in_mix(q) * P, (place_in_mix(q) + 1) * P)
                    dst = chunks(wait_filled(act, ("T0", q)))
                    drain(("T0", q), [(qT[:, :, at], dst[:, 0:6, :]), (kT[:, 0:2, at], dst[:, 6:8, :])])
                    dst = chunks(wait_filled(act, ("T1", q)))
                    drain(("T1", q), [(kT[:, 2, at], dst[:, 0, :]), (hT[:, 0:2, at], dst[:, 1:3, :])])
                elif kind == "att":
                    attention(*a)
                elif kind == "four":
                    m = a[0]
                    for b, q in enumerate(BLOCKS[m]):
                        dst = wait_filled(act, ("FY", q))
                        drain(("FY", q), [(fy[:, b, :], dst[:, 0, :])])
                    dst = wait_filled(act, ("FF", m))
                    drain(("FF", m), [(fT[:, :, 0:width(m)], dst[:, :, 0:width(m)])])
                    for b, q in enumerate(BLOCKS[m]):
                        dst = wait_filled(act, ("FO", q))
                        drain(("FO", q), [(qkv[:, b, FN:IN_W], dst[:, 0, 0:IN_W - FN])])
                elif kind == "oT":
                    q = a[0]
                    at = slice(place_in_mix(q) * P, (place_in_mix(q) + 1) * P)
                    dst = wait_filled(act, ("OT", q))
                    drain(("OT", q), [(hT[:, :, at], chunks(dst))])
                elif kind in ("gate", "ln2"):
                    key = ("G", BLOCKS[a[0]][0], 1) if kind == "gate" else ("G", a[0], 2)
                    if ln_before(step):
                        act.wait_ge(ln_done, ln_before(step))
                    if routes_before(step):
                        act.wait_ge(route_ready, routes_before(step))
                    dst = wait_filled(act, key)
                    drain(key, [(gate_b, dst[:, :, :])])
                    if kind == "ln2":
                        square_root(("ln2", a[0]))
                elif kind == "ln1":
                    square_root(("ln1", a[0]))
                elif kind == "h2":
                    q = a[0]
                    modulate(("X2", q), q, 1)
                    if q >= 3:
                        act.wait_ge(ln_done, LN[(q - 3, 2)])
                    dst = wait_filled(act, ("H2", q))
                    drain(("H2", q), [(h_tok[:, q % 3, :].rearrange("p (a n) -> p a n", a=2), dst[:, :, :])])
                elif kind == "wq":
                    m, n = a
                    nb, t = len(BLOCKS[m]), width(m)
                    if n < R_H:
                        dst = wait_filled(act, ("WQ", m, n))
                        drain(("WQ", m, n), [(qpT[:, n % 2, :, 0:t], dst[:, :, 0:t])])
                    if n == 1:
                        act.wait_ge(ln_done, ln_before(step))
                        if not MIXES[m][1]:
                            act.wait_ge(kv_stored, 64 * (MIXES[m][0] + 1))
                    if n:
                        dst = wait_filled(act, ("SC", m, n - 1))
                        drain(("SC", m, n - 1), [(scores[:, 0:nb, (n - 1) * TW:n * TW], dst[:, 0:nb, 0:TW])])
                elif kind == "pick" and a[1] == 1:
                    act.wait_ge(best_ready, ROUTE[a[0]])
                    nc.scalar.activation(gate_e[:, :, :], gate_e[:, :, :], ACT.Exp).then_inc(gate_exp, 1)

        @block.vector
        def _(dve):
            links = [0]

            def link(ins):
                links[0] += 1
                ins.then_inc(dve_chain, 1)
                dve.wait_ge(dve_chain, links[0])

            def spread(ap, shape):
                return ap.to_broadcast(shape)

            def maxima(q, u):
                m, b = mix_of(q), place_in_mix(q)
                nk = 3 * P if MIXES[m][1] else P
                dst = wait_filled(dve, ("A", q, u))
                if MIXES[m][1] and u < 2:
                    link(nc.vector.tensor_tensor(dst[:, :, 0:2 * P], dst[:, :, 0:2 * P], bias[:, b, 2 * u:2 * u + 2, :], ALU.add))
                link(nc.vector.reduce_max(maxes[:, :], dst[:, :, 0:nk], AX.X))
                nc.vector.tensor_scalar(neg_max[:, u % 2, :], maxes[:, :], -SCALE, None, ALU.mult).then_inc(neg_max_ready, 1)
                dve.wait_ge(neg_max_ready, UNIT[(q, u)])

            def attention(q, u0, u1):
                b = place_in_mix(q)
                maxima(q, u0)
                for u in range(u0, u1):
                    if u + 1 < u1:
                        maxima(q, u + 1)
                    wait_drained(dve, ("A", q, u))
                    link(nc.vector.reciprocal(inv_sum[:, :], row_sum[:, u % 2, :]))
                    dst = wait_filled(dve, ("O", q, u))
                    if u < 2:
                        out = qkv[:, b, 2 * u * HD:(2 * u + 2) * HD].rearrange("p (i d) -> p i d", i=2)
                    else:
                        out = qkv[:, b, G_Q:G_Q + Q_H * HD].rearrange("p (g i d) -> p i g d", g=2, i=4)[:, u - 2]
                    nc.vector.tensor_tensor(out, dst[:, 0, 0:2 * HD].rearrange("p (i d) -> p i d", i=2),
                                            spread(inv_sum[:, :].unsqueeze(2), [P, 2, HD]), ALU.mult)\
                        .then_inc(drained_by_dve, 1)
                    wait_drained(dve, ("O", q, u))

            def layer_norm(q, which):
                slot, l = q % 3, q // 3
                x = x_tok[:, slot, :]
                key = (q, which)
                zz = z.rearrange("p (a n) -> p a n", a=2)
                wait_drained(dve, ("G", BLOCKS[mix_of(q)][0] if which == 1 else q, which))
                if which == 1:
                    dst = wait_filled(dve, ("Z", q))
                    if l == 0:
                        dve.wait_ge(x_landed, 48)
                    nc.vector.tensor_tensor(zz, dst[:, :, :], gate_b, ALU.mult).then_inc(drained_by_dve, 1)
                    dve.wait_ge(drained_by_dve, DRAINED_BY_DVE[("Z", q)])
                else:
                    dve.wait_ge(v_used, RING + PER_TOKEN * (q + 1))
                    nc.vector.tensor_tensor(zz, acc[:, :, :], gate_b, ALU.mult).then_inc(acc_drained, 1)
                    dve.wait_ge(acc_drained, q + 1)
                link(nc.vector.scalar_tensor_tensor(out=z, in0=x, scalar=ALPHA, in1=z, op0=ALU.mult, op1=ALU.add))
                nc.vector.bn_stats(stats[:, 0, :], z[:, 0:512])
                link(nc.vector.bn_stats(stats[:, 1, :], z[:, 512:D]))
                link(nc.vector.bn_aggr(mean_var[:, :], stats[:, :, :]))
                nc.vector.tensor_scalar(root_in[:, 0:1], mean_var[:, 1:2], LN_EPS, None, ALU.add).then_inc(root_in_ready, 1)
                n = ROOTS[("ln1" if which == 1 else "ln2", q)]
                dve.wait_ge(root_ready, n)
                link(nc.vector.reciprocal(rroot[:, 0:1], root[:, 0:1]))
                link(nc.vector.tensor_scalar(z, z, mean_var[:, 0:1], rroot[:, 0:1], ALU.subtract, ALU.mult))
                dve.wait_ge(ln_rows_landed, 32 * LN[key])
                link(nc.vector.tensor_tensor(z, z, ln_rows[:, 0, :], ALU.mult))
                nc.vector.tensor_tensor(x, z, ln_rows[:, 1, :], ALU.add).then_inc(ln_done, 1)
                dve.wait_ge(ln_done, LN[key])

            def rms_norm_and_rotate(q):
                l, latent, b = q // 3, q % 3 > 0, place_in_mix(q)
                dve.wait_ge(squares_ready, NORM[q])
                link(nc.vector.reduce_sum(root_in[:, :], squares.rearrange("p (h d) -> p h d", d=HD), AX.X))
                nc.vector.tensor_scalar(root_in[:, :], root_in[:, :], 1.0 / HD, RMS_EPS, ALU.mult, ALU.add).then_inc(root_in_ready, 1)
                dve.wait_ge(root_ready, ROOTS[("norm", q)])
                link(nc.vector.reciprocal(rroot[:, :], root[:, :]))
                x = qkv[:, b, G_Q:G_V].rearrange("p (h d) -> p h d", d=HD)
                t1, t2, t3 = (t.rearrange("p (h d) -> p h d", d=HD) for t in (turned, turned2, squares))
                out = [x[:, 0:Q_H].rearrange("p (i g) d -> p g i d", g=KV_H), x[:, Q_H:]]

                def grouped(t):
                    return [t[:, 0:Q_H].rearrange("p (g i) d -> p g i d", g=KV_H), t[:, Q_H:]]

                link(nc.vector.tensor_tensor(t1, x, spread(rroot[:, :].unsqueeze(2), [P, RMS_HEADS, HD]), ALU.mult))
                by = [spread(gains[:, l, 0, :].unsqueeze(1), [P, Q_H, HD]), spread(gains[:, l, 1, :].unsqueeze(1), [P, KV_H, HD])]
                nc.vector.tensor_tensor(t1[:, 0:Q_H], t1[:, 0:Q_H], by[0], ALU.mult)
                link(nc.vector.tensor_tensor(t1[:, Q_H:], t1[:, Q_H:], by[1], ALU.mult))
                if latent:
                    nc.vector.tensor_tensor(t2, t1, spread(rope[:, b, 0, :].unsqueeze(1), [P, RMS_HEADS, HD]), ALU.mult)
                    for half in range(2):
                        for y in range(2):
                            to = slice(32 * half + 16 * y, 32 * half + 16 * y + 16)
                            of = slice(32 * half + 16 * (1 - y), 32 * half + 16 * (1 - y) + 16)
                            last = nc.vector.tensor_tensor(t3[:, :, to], t1[:, :, of],
                                                           spread(rope[:, b, 1, to].unsqueeze(1), [P, RMS_HEADS, 16]), ALU.mult)
                    link(last)
                    for d, s2, s3 in zip(out, grouped(t2), grouped(t3)):
                        last = nc.vector.tensor_tensor(d, s2, s3, ALU.add)
                else:
                    for d, s1 in zip(out, grouped(t1)):
                        last = nc.vector.tensor_copy(d, s1)
                last.then_inc(norm_ready, 1)

            def top_sixteen(groups):
                for v, out, _ in groups:
                    last = nc.vector.max(out=out[:, 0:8], in_=v)
                link(last)
                for v, out, at in groups:
                    last = nc.vector.max_index(out=at[:, 0:8], in_max=out[:, 0:8], in_values=v)
                link(last)
                for v, out, _ in groups:
                    last = nc.vector.match_replace(out=v, in_to_replace=out[:, 0:8], in_values=v, imm_value=LOWEST)
                link(last)
                for v, out, _ in groups:
                    last = nc.vector.max(out=out[:, 8:16], in_=v)
                link(last)
                for v, out, at in groups:
                    last = nc.vector.max_index(out=at[:, 8:16], in_max=out[:, 8:16], in_values=v)
                link(last)

            def pick_experts(q, part):
                l, slot = q // 3, q % 3
                c4 = cand.rearrange("p (h a b) -> p h a b", h=R_H, a=TOPK)
                top4 = top_s[:, :, :].rearrange("p (h f) k -> p h f k", f=2)
                shape = [P, R_H, TOPK, TOPK]
                top_f = scores[:, place_in_mix(q), 0:2 * R_H * TOPK].rearrange("p (h f k) -> p h f k", f=2, k=TOPK)
                if part == 0:
                    link(nc.vector.tensor_tensor(c4, spread(top4[:, :, 0, :].unsqueeze(3), shape),
                                                 spread(top4[:, :, 1, :].unsqueeze(2), shape), ALU.add))
                if part < 2:
                    flat = cand.rearrange("p (h n) -> p h n", h=R_H)
                    heads = range(4 * part, 4 * part + 4)
                    top_sixteen([(flat[:, h], best_s[:, h], best_j[:, h]) for h in heads])
                if part == 1:
                    nc.vector.tensor_tensor(gate_e[:, :, :], best_s[:, :, :], spread(best_s[:, :, 0:1], [P, R_H, TOPK]),
                                            ALU.subtract).then_inc(best_ready, 1)
                    link(nc.vector.tensor_copy(top_f, top_i[:, :, :].rearrange("p (h f) k -> p h f k", f=2)))
                if part >= 2:
                    f = part - 2
                    j = best_j[:, :, :].rearrange("p h k -> p (h k)")
                    hit = cand.rearrange("p (n a) -> p n a", a=TOPK)
                    op, by = ((ALU.logical_shift_right, 4), (ALU.bitwise_and, 15))[f]
                    link(nc.vector.tensor_scalar(half_j[:, :], j, by, None, op))
                    link(nc.vector.tensor_copy(half_f[:, :], half_j[:, :]))
                    link(nc.vector.tensor_tensor(hit, spread(half_f[:, :].unsqueeze(2), [P, PER_TOKEN, TOPK]),
                                                 spread(iota.unsqueeze(1), [P, PER_TOKEN, TOPK]), ALU.is_equal))
                    link(nc.vector.tensor_tensor(c4, c4, spread(top_f[:, :, f, :].unsqueeze(2), shape), ALU.mult))
                    link(nc.vector.reduce_sum(picked[:, f, :], hit, AX.X))
                if part < 3:
                    return
                link(nc.vector.scalar_tensor_tensor(out=picked[:, 0, :], in0=picked[:, 0, :], scalar=float(KEYS),
                                                    in1=picked[:, 1, :], op0=ALU.mult, op1=ALU.add))
                link(nc.vector.tensor_scalar(experts[:, slot, :], picked[:, 0, :], float(l * EXPERTS), None, ALU.add))
                dve.wait_ge(gate_exp, ROUTE[q])
                link(nc.vector.reduce_sum(gate_n[:, :], gate_e[:, :, :], AX.X))
                link(nc.vector.reciprocal(gate_n[:, :], gate_n[:, :]))
                nc.vector.tensor_tensor(gates[:, slot, :].rearrange("p (h k) -> p h k", h=R_H), gate_e[:, :, :],
                                        spread(gate_n[:, :].unsqueeze(2), [P, R_H, TOPK]), ALU.mult).then_inc(route_ready, 1)
                dve.wait_ge(route_ready, ROUTE[q])

            def gate_on_diagonals(key):
                q, which = key
                part = PART_G1 if which == 1 else PART_G2
                wait_drained(dve, ("MD", q // 3, part))
                wait_filled(dve, ROUNDS[ROUND[("G", q, which)] - 1])
                column = mod_cols[:, q // 3, part, :, int(q % 3 > 0)]
                nc.vector.tensor_tensor(z.rearrange("p (c n) -> p c n", c=NC), spread(ident.unsqueeze(1), [P, NC, P]),
                                        spread(column.unsqueeze(2), [P, NC, P]), ALU.mult).then_inc(gate_diag_ready, 1)

            def expert_dots(q, h0, h1):
                slot_q = q % 3
                if h0 == 0:
                    wait_drained(dve, ("H2", q))
                    if q == 0:
                        dve.sem_inc(u_used, RING)

                def weigh(p, half, at):
                    dve.wait_ge(gelu_ready, p * 2 + half + 1)
                    nc.vector.tensor_tensor(weight[:, half, :], gelu[:, half, :], gates[:, slot_q, bass.ds(at, G)], ALU.mult)\
                        .then_inc(weight_ready, 1)

                def dot(p, half):
                    for j in range(G):
                        slot = half * G + j
                        dve.wait_ge(u_used, p * RING + slot + RING)
                        dve.wait_ge(u_landed[slot], p * 16 + 16)
                        nc.vector.tensor_tensor_reduce(out=products[:, :], in0=u_rows[:, slot, :], in1=h_tok[:, slot_q, :],
                                                       scale=1.0, scalar=0.0, op0=ALU.mult, op1=ALU.add,
                                                       accum_out=dots[:, half, j:j + 1]).then_inc(u_used, 1)

                first = q * GROUPS // 2

                def turn(p, half):
                    weigh(p - 1 if half == 0 else p, 1 - half, (p - first) * RING + half * G - G)
                    dot(p, half)

                if h0 == 0:
                    dot(first, 0)
                turns_of(dve, q, max(h0, 1), min(h1, GROUPS), turn)
                if h1 == TURNS:
                    weigh(first + GROUPS // 2 - 1, 1, PER_TOKEN - G)

            dve.wait_ge(consts_landed, 16 * N_CONST_DMAS)
            dve.wait_ge(cond_exp, 1)
            link(nc.vector.tensor_scalar(cond_e[:, :, :], cond_e[:, :, :], 1.0, None, ALU.add))
            link(nc.vector.reciprocal(cond_e[:, :, :], cond_e[:, :, :]))
            nc.vector.tensor_tensor(cond_s[:, :, :], cond[:, :, :], cond_e[:, :, :], ALU.mult).then_inc(cond_ready, 1)
            for step in SCHEDULE:
                kind, a = step[0], step[1:]
                if kind == "gather":
                    expert_dots(*a)
                elif kind == "mod":
                    l, c = a
                    dst = wait_filled(dve, ("MD",) + a)
                    nc.vector.scalar_tensor_tensor(out=mod_cols[:, l, c, :, :], in0=dst[:, 0, 0:2 * NC].rearrange("p (c k) -> p c k", k=2),
                                                   scalar=float(c in (PART_SC1, PART_SC2)),
                                                   in1=spread(b_mod[:, l, c, :].unsqueeze(2), [P, NC, 2]),
                                                   op0=ALU.add, op1=ALU.add).then_inc(drained_by_dve, 1)
                elif kind == "bias":
                    half = a[1]
                    dst = wait_filled(dve, ("B",) + a)
                    for b in range(2):
                        for r in range(2):
                            part = slice(64 * r, 64 * r + 64)
                            row = 2 * b + r
                            psum = dst[part, :, 0:16 * NA_H * ROW_DIFFS].rearrange("p k (c x) -> p x k c", c=16)
                            mask = window[part, 32 * half:32 * half + 32].rearrange("p (k c) -> p k c", k=2)
                            for h in range(NA_H):
                                out = bias[part, b, h, :].rearrange("p (j c) -> p j c", j=4)[:, :, 32 * half:32 * half + 32]
                                at = h * ROW_DIFFS + 3 - row
                                last = nc.vector.tensor_tensor(out.rearrange("p j (k c) -> p j k c", k=2), psum[:, at:at + 4],
                                                               spread(mask.unsqueeze(1), [GRID_W, 4, 2, 16]), ALU.add)
                    last.then_inc(drained_by_dve, 1)
                    wait_drained(dve, ("B",) + a)
                elif kind == "norm":
                    rms_norm_and_rotate(a[0])
                elif kind == "att":
                    attention(*a)
                elif kind == "ln1":
                    layer_norm(a[0], 1)
                elif kind == "gate":
                    gate_on_diagonals((BLOCKS[a[0]][0], 1))
                elif kind == "ln2":
                    gate_on_diagonals((a[0], 2))
                    layer_norm(a[0], 2)
                elif kind == "top":
                    q, first = a
                    m, b = mix_of(q), place_in_mix(q)
                    wait_drained(dve, ("SC", m, first // 2 + 3))
                    top_sixteen([(scores[:, b, n * KEYS:(n + 1) * KEYS], top_s[:, n], top_i[:, n])
                                 for n in range(first, first + R_H)])
                elif kind == "pick":
                    pick_experts(*a)


def constants():
    import numpy as np

    def place(name, rows, value):
        a, b = CONST[name]
        out[rows, a:b] = np.asarray(value, np.float64).reshape(out[rows, a:b].shape).astype(np.float32)

    out = np.zeros((P, CONST_W), np.float32)
    place("ident", slice(None), np.eye(P))
    place("ones", slice(None), np.ones((P, P)))
    pos = np.arange(2 * P)
    inv = (1.0 / (np.float32(10000.0) ** (np.arange(16, dtype=np.float32) / np.float32(16)))).astype(np.float32)
    table = np.zeros((2 * P, 2, HD))
    for half, where in enumerate((pos // GRID_W, pos % GRID_W)):
        angle = (where.astype(np.float32)[:, None] * inv).astype(np.float64)
        at = 32 * half
        table[:, 0, at:at + 16] = table[:, 0, at + 16:at + 32] = np.cos(angle)
        table[:, 1, at:at + 16] = -np.sin(angle)
        table[:, 1, at + 16:at + 32] = np.sin(angle)
    place("rope", slice(None), table.reshape(2, P, 2 * HD).transpose(1, 0, 2))

    def dft(n):
        angle = 2 * np.pi * (np.outer(np.arange(n), np.arange(n)) % n) / n
        return np.stack([np.cos(angle), -np.sin(angle)]) / np.sqrt(n)

    place("dft_ctx", slice(None), dft(P).transpose(1, 0, 2))
    place("dft_lat", slice(None), dft(2 * P).reshape(2, 2, P, 2 * P).transpose(2, 1, 0, 3))
    channels = np.zeros((2, HD, 2, 2, HD))
    for g in range(2):
        channels[g, :, 0, g] = dft(HD)[0]
        channels[g, :, 1, g] = -dft(HD)[1]
    place("dft_ch", slice(None), channels.reshape(P, 2 * P))
    col = np.arange(GRID_W)
    start = np.clip(col - 8, 0, GRID_W - 16)
    inside = (col[None] >= start[:, None]) & (col[None] < start[:, None] + 16)
    place("window", slice(None), np.tile(np.where(inside, 0.0, -1e30), (2, 1)))
    shifts = np.zeros((RPB_COLS, 2 * GRID_W))
    shifts[np.arange(RPB_COLS), 78 - np.arange(RPB_COLS)] = 1.0 / SCALE
    place("shift", slice(0, RPB_COLS), shifts)
    place("iota", slice(None), np.tile(np.arange(TOPK), (P, 1)))
    return out


def kernel(**inputs):
    import concourse.bacc as bacc
    import numpy as np
    from concourse.bass_utils import run_bass_kernel_spmd

    a = {k: np.asarray(v) for k, v in inputs.items()}
    n = DEPTH
    wf = np.zeros((2, HD, n, 2, 2, HD), np.float32)
    f = a["w_fourier"].reshape(n, 2, 2, HD, HD)
    for g in range(2):
        wf[g, :, :, :, g] = f[:, :, g].transpose(2, 0, 1, 3)

    def keys_by_channel(k):
        return k.transpose(0, 2, 3, 1).reshape(n, -1, P, P)

    arrays = {
        "x_prompt": a["x_prompt"], "x_sample": a["x_sample"], "consts": constants(),
        "cond": np.stack([a["c_ctx"], a["c"][0]]).reshape(2, NC, P).transpose(2, 1, 0),
        "rpb": a["na_rpb"].transpose(3, 0, 1, 2),
        "gains": np.stack([a["q_gain"], a["k_gain"]], axis=1),
        "wf": wf.reshape(P, n, 2, P),
        "w_mod": a["w_mod"], "b_mod": a["b_mod"].reshape(n, 6, NC, P).transpose(3, 0, 1, 2), "w_in": a["w_in"], "w_out": a["w_out"], "peer_wq": a["peer_wq"],
        "sub_keys": a["peer_subkeys"].transpose(0, 4, 1, 2, 3).reshape(n, P, 2 * R_H, KEYS),
        "ctx_kT": np.concatenate([keys_by_channel(a["cache_na_k"][0]), keys_by_channel(a["cache_gqa_k"][0])],
                                 axis=1).transpose(0, 2, 1, 3),
        "ctx_v": np.concatenate([a["cache_na_v"][0].reshape(n, P, -1), a["cache_gqa_v"][0].reshape(n, P, -1)], axis=2),
        "ln1_g": a["ln1_g"], "ln1_b": a["ln1_b"], "ln2_g": a["ln2_g"], "ln2_b": a["ln2_b"],
        "peer_u": a["peer_u"].reshape(n * EXPERTS, D), "peer_v": a["peer_v"].reshape(n * EXPERTS, D),
    }
    outs = {"y_prompt": (1, P, D), "y_sample": (1, 2 * P, D), "new_na_k": (n, P, 256), "new_na_v": (n, P, 256),
            "new_gqa_k": (n, P, 128), "new_gqa_v": (n, P, 128)}
    nc = bacc.Bacc("TRN2", target_bir_lowering=False, num_devices=1)
    arrays = {f"in_{k}": np.ascontiguousarray(v) for k, v in arrays.items()}
    i = {k[3:]: nc.dram_tensor(k, v.shape, mybir.dt.from_np(v.dtype), kind="ExternalInput").ap() for k, v in arrays.items()}
    o = {k: nc.dram_tensor(f"out_{k}", s, F32, kind="ExternalOutput").ap() for k, s in outs.items()}
    hybrid_step(nc, i, o)
    got = run_bass_kernel_spmd(nc, [arrays], core_ids=[0]).results[0]
    r = {k: got[f"out_{k}"] for k in outs}
    return (r["y_prompt"], r["y_sample"], r["new_na_k"].reshape(1, n, P, NA_H, HD), r["new_na_v"].reshape(1, n, P, NA_H, HD),
            r["new_gqa_k"].reshape(1, n, P, KV_H, HD), r["new_gqa_v"].reshape(1, n, P, KV_H, HD))
```

```python
from contextlib import ExitStack

import concourse.bass as bass
from concourse import mybir

F32 = mybir.dt.float32
BF16 = mybir.dt.bfloat16
U32 = mybir.dt.uint32
ALU = mybir.AluOpType
ACT = mybir.ActivationFunctionType
AX = mybir.AxisListType

P = 128
DEPTH = 2
D = 1024
NC = D // P
HD = 64
NA_H, Q_H, KV_H = 4, 8, 2
NA_Q, NA_K, NA_V, G_Q = 0, 256, 512, 768
G_K, G_V, FN = 1280, 1408, 1536
IN_W = 1792
RMS_HEADS = Q_H + KV_H
GRID_W = 64
EXPERTS = 16384
R_H, TOPK, KEYS = 8, 16, 128
PER_TOKEN = R_H * TOPK
ALPHA = (2 * DEPTH) ** 0.25
LN_EPS, RMS_EPS = 1e-5, 1e-6
SCALE = HD ** -0.5
LOWEST = -3.0e38

QUADRANT = 32
GROUPS_OF_PE = P // QUADRANT
TW = 256
WSLOTS = 3
SK_SLOTS = 3
G = 4
RING = 2 * G
GROUPS = PER_TOKEN // G

MIXES = [(0, 0), (0, 1), (1, 0), (1, 1)]
BLOCKS = [[0], [1, 2], [3], [4, 5]]
PART_SH1, PART_SC1, PART_G1, PART_SH2, PART_SC2, PART_G2 = range(6)
UNITS = 6


def modulation_steps(l, part):
    return [("mod", l, part, t) for t in range(D // TW + 1)]


def attention_steps(m):
    return [("att", m, n) for n in range(UNITS * len(BLOCKS[m]) + 2)]


TO_NORM = list(range(G_Q // TW, -(-G_V // TW)))
PROJ_ORDER = TO_NORM + [n for n in range(IN_W // TW) if n not in TO_NORM]


def mix_start(m):
    l, latent = MIXES[m]
    qs = BLOCKS[m]
    steps = [("xT", q) for q in qs] + [("proj", m, n) for n in TO_NORM]
    between = [("norm", q) for q in qs] + ([("bias", l)] if latent else [])
    for n in PROJ_ORDER[len(TO_NORM):]:
        steps += between[:1] + [("proj", m, n)]
        between = between[1:]
    return steps


def mix_middle(m):
    l, latent = MIXES[m]
    qs = BLOCKS[m]
    steps = [("qkT", q) for q in qs]
    att = attention_steps(m)
    for n in range(3):
        steps += att[2 * n:2 * n + 2] + [("four", m, n)]
    return steps + att[6:] + ([] if latent else [("kvout", qs[0])]) + [("oT", q) for q in qs]


def mix_end(m):
    qs = BLOCKS[m]
    steps = [("gate", m)] + [("outp", m, n) for n in range(D // TW)]
    if len(qs) == 1:
        return steps + [(kind, qs[0], n) for kind in ("ln1", "h2") for n in range(2)]
    a, b = qs
    return steps + [("ln1", a, 0), ("ln1", a, 1), ("h2", a, 0), ("ln1", b, 0), ("h2", a, 1), ("ln1", b, 1),
                    ("h2", b, 0), ("h2", b, 1)]


def query_steps(m):
    q = BLOCKS[m][0]
    steps = []
    for n in range(R_H + 1):
        steps.append(("wq", m, n))
        if n and n % 2 == 0:
            steps += [("top", q, n // 2 - 1), ("pick", q, n // 2 - 1)]
    return steps + [("pick", q, 4), ("pick", q, 5)]


def route_steps(q):
    return [s for n in range(4) for s in (("top", q, n), ("pick", q, n))] + [("pick", q, 4), ("pick", q, 5)]


COST = {"mod": (3, 3), "bias": (2, 2), "xT": (3, 3), "proj": (4, 6), "norm": (4, 6), "qkT": (2, 2), "att": (3, 12),
        "four": (0, 0), "kvout": (0, 0), "oT": (1, 1), "gate": (3, 3), "gate2": (0, 0), "outp": (4, 7),
        "ln1": (3, 3), "h2": (4, 4), "wq": (4, 8), "top": (4, 4), "pick": (5, 5), "ln2": (4, 4)}
TURNS = GROUPS + 2


def cost(step):
    by_mix = step[0] in ("proj", "att", "outp", "wq", "four")
    return COST[step[0]][by_mix and len(BLOCKS[step[1]]) - 1] + 3 * (step[0] == "pick" and step[2] >= 4)


def beside(q, steps, behind=0):
    out, at, passed = [], 0, 0
    if q:
        out = [("gather", q, 0, 2), ("ln2", q - 1, 0), ("gather", q, 2, 3), ("ln2", q - 1, 1), ("gather", q, 3, 4)]
        at = 4
        if q == BLOCKS[2][0]:
            out = [("gather", q, 0, 1), ("ln2", q - 1, 0), ("gather", q, 1, 2), ("ln2", q - 1, 1)]
            at = 2
    ahead = at
    whole = sum(cost(s) for s in steps)
    for step in steps:
        until = ahead + (TURNS - ahead - behind) * passed // max(whole, 1)
        if until > at:
            out.append(("gather", q, at, until))
            at = until
        out.append(step)
        passed += cost(step)
    late = max(at, TURNS - 2)
    return out + [("gather", q, at, late)] * (at < late) + [("gate2", q), ("gather", q, late, TURNS)]


def filled_in(steps, fill, counts):
    out = []
    for step in steps:
        out.append(step)
        for _ in range(counts.get(step[0], 0)):
            if fill:
                out.append(fill.pop(0))
    return out


FILL = {"kvout": 1, "qkT": 1, "att": 2, "four": 1, "ln1": 3, "h2": 1, "top": 2, "pick": 5}


def build_schedule():
    s = modulation_steps(0, PART_SH1) + modulation_steps(0, PART_SC1)
    fill = [t for part in range(PART_G1, 6) for t in modulation_steps(0, part)]
    fill += [t for part in range(6) for t in modulation_steps(1, part)]
    s += filled_in(mix_start(0) + mix_middle(0), fill, FILL)
    queries = query_steps(0)
    last = queries.index(("wq", 0, R_H))
    s += filled_in(mix_end(0), fill, FILL) + queries[:last + 1] + filled_in(queries[last + 1:], fill, FILL)
    s += beside(0, mix_start(1) + mix_middle(1) + mix_end(1) + query_steps(1), 2)
    s += beside(1, route_steps(2) + fill + mix_start(2))
    s += beside(2, mix_middle(2) + mix_end(2) + query_steps(2), 3)
    s += beside(3, mix_start(3) + mix_middle(3) + mix_end(3) + query_steps(3), 2)
    s += beside(4, route_steps(5), 3)
    s += beside(5, []) + [("ln2", 5, 0), ("ln2", 5, 1)]
    return s


SCHEDULE = build_schedule()


def units_of(m, n):
    units = [(q, u) for q in BLOCKS[m] for u in range(UNITS)]
    return [units[k] if 0 <= k < len(units) else None for k in (n - 2, n - 1, n)]


def rounds_of(step):
    kind, a = step[0], step[1:]
    if kind == "mod":
        l, part, t = a
        return ([("MR",) + a] if t < D // TW else []) + ([("MC", l, part, t - 1)] if t else [])
    if kind == "xT":
        return [("X", a[0])]
    if kind == "proj":
        return [("J",) + a]
    if kind == "qkT":
        return [("T0", a[0]), ("T1", a[0])]
    if kind == "att":
        return [(name,) + unit for name, unit in zip(("O", "PT", "A"), units_of(*a)) if unit]
    if kind == "four":
        m, part = a
        qs = BLOCKS[m]
        return ([("FY", q) for q in qs], [("FF", m)], [("FO", q) for q in qs])[part]
    if kind == "oT":
        return [("OT", a[0])]
    if kind == "gate":
        return [("G", BLOCKS[a[0]][0], 1)]
    if kind == "outp":
        return [("Z", q) for q in BLOCKS[a[0]]] if a[1] == 0 else []
    if kind == "h2":
        return [(("X2", "H2")[a[1]], a[0])]
    if kind == "wq":
        m, n = a
        return ([("WQ", m, n)] if n < R_H else []) + ([("SC", m, n - 1)] if n else [])
    if kind == "gate2":
        return [("G", a[0], 2)]
    return []


ROUNDS = [r for s in SCHEDULE for r in rounds_of(s)]
PAIRS = 3
ROUND = {r: n for n, r in enumerate(ROUNDS)}
BY_DVE = {"O", "Z"}
BY_TILE = {"MR", "J", "Z", "SC"}


def numbered(kinds, keys):
    return {k: n + 1 for n, k in enumerate(k for s in SCHEDULE if s[0] in kinds for k in keys(s))}


def counted(rounds):
    return {r: n + 1 for n, r in enumerate(rounds)}


DRAINED_BY_DVE = counted(r for r in ROUNDS if r[0] in BY_DVE)
DRAINED_BY_ACT = counted(r for r in ROUNDS if r[0] not in BY_DVE)
FILLED = counted(r for r in ROUNDS if r[0] not in BY_TILE)
LN = numbered(("ln1", "ln2"), lambda s: [(s[1], 1 if s[0] == "ln1" else 2)] if s[2] else [])
NORM = numbered(("norm",), lambda s: [s[1]])
ROOTS = numbered(("norm", "ln1", "ln2"), lambda s: [] if s[0] != "norm" and s[2] else [(s[0], s[1])])
UNIT = numbered(("att",), lambda s: [unit for unit in units_of(s[1], s[2])[2:] if unit])
ROUTE = numbered(("pick",), lambda s: [s[1]] if s[2] == 5 else [])
GATE = numbered(("gate", "gate2"), lambda s: [(BLOCKS[s[1]][0], 1) if s[0] == "gate" else (s[1], 2)])
TILES = numbered(("mod", "proj", "outp", "wq"),
                 lambda s: [] if s[0] == "mod" and s[3] == D // TW or s[0] == "wq" and s[2] == R_H else [s])


def ln_before(step):
    return sum(s[0] in ("ln1", "ln2") and s[2] == 1 for s in SCHEDULE[:SCHEDULE.index(step)])


def routes_before(step):
    return sum(s[0] == "pick" and s[2] == 5 for s in SCHEDULE[:SCHEDULE.index(step)])


def mix_of(q):
    return next(m for m in range(4) if q in BLOCKS[m])


def place_in_mix(q):
    return q - BLOCKS[mix_of(q)][0]


def width(m):
    return P * len(BLOCKS[m])


def last_tile(key):
    kind = key[0]
    if kind == "Z":
        return ("outp", mix_of(key[1]), 3)
    return ({"MR": "mod", "J": "proj", "SC": "wq"}[kind],) + key[1:]


EARLY_TILES = sum(s in TILES for s in SCHEDULE[:SCHEDULE.index(("xT", BLOCKS[1][0]))])
EARLY_SLOTS = 2 * RING * D // (NC * TW)


def slot_of(n):
    if n > EARLY_TILES:
        return (n - 1) % WSLOTS
    return (n - 1) % (WSLOTS + EARLY_SLOTS)


def last_in_slot(n):
    return max((v for v in range(1, n) if slot_of(v) == slot_of(n)), default=0)


def tile_arrival(key):
    n = TILES[key]
    slot = slot_of(n)
    return slot, 16 * sum(2 if k[0] == "wq" else 1 for k, v in TILES.items() if slot_of(v) == slot and v <= n)


CONST = {}
_at = 0
for _name, _n in (("ident", P), ("ones", P), ("rope", 2 * 2 * HD), ("dft_ctx", 2 * P), ("dft_lat", 2 * 2 * 2 * P),
                  ("dft_ch", 2 * P), ("window", GRID_W), ("halves", 2), ("iota", TOPK), ("zero", P)):
    CONST[_name] = (_at, _at + _n)
    _at += _n
CONST_W = _at
NA_WIN_H, NA_WIN_W = 8, 16
ROWS_MAX_DIFF = 3


def hybrid_step(nc, i, o):
    ctx = ExitStack()
    with ctx:
        def sb(name, shape, dt=F32):
            return ctx.enter_context(nc.sbuf_tensor(name, shape, dt))

        def sem(name):
            return ctx.enter_context(nc.semaphore(name))

        u_rows = sb("u_rows", [P, RING, D])
        v_rows = sb("v_rows", [P, RING, D])
        wtiles = sb("wtiles", [P, WSLOTS, NC, TW])
        sktiles = sb("sktiles", [P, SK_SLOTS, 2, KEYS])
        x_tok = sb("x_tok", [P, 3, D])
        h_tok = sb("h_tok", [P, 3, D])
        hT = sb("hT", [P, NC, 2 * P])
        mod_cols = sb("mod_cols", [P, DEPTH, 6, NC, 2])
        b_mod = sb("b_mod_cols", [P, DEPTH, 6, NC])
        rows = sb("rows", [P, 2 * D])
        ln_rows = rows[:, :].rearrange("p (r n) -> p r n", r=2)
        bias = rows[:, :].rearrange("p (b h n) -> p b h n", b=2, h=NA_H)
        arena = sb("arena", [P, 7424])
        qT = sb("qT", [P, 6, 2 * P])
        kT = sb("kT", [P, 3, 3 * P])
        consts = sb("consts", [P, CONST_W])
        mod_row = sb("mod_row", [P, 2, TW])
        gains = sb("gains", [P, DEPTH, 2, HD])
        wf = sb("wf", [P, DEPTH, 2, P])
        v_ctx = sb("v_ctx", [P, (NA_H + KV_H) * HD])
        cond = sb("cond", [P, NC, 2])
        cond_e = sb("cond_e", [P, NC, 2])
        cond_s = sb("cond_s", [P, NC, QUADRANT])
        stats = sb("stats", [P, 2, 6])
        mean_var = sb("mean_var", [P, 2])
        root_in = sb("root_in", [P, RMS_HEADS])
        root = sb("root", [P, RMS_HEADS])
        rroot = sb("rroot", [P, RMS_HEADS])
        maxes = sb("maxes", [P, 2])
        neg_max = sb("neg_max", [P, 2, 2])
        row_sum = sb("row_sum", [P, 2, 2])
        inv_sum = sb("inv_sum", [P, 2])
        top_s = sb("top_s", [P, 2 * R_H, TOPK])
        top_i = sb("top_i", [P, 2 * R_H, TOPK], U32)
        best_s = sb("best_s", [P, R_H, TOPK])
        best_j = sb("best_j", [P, R_H, TOPK], U32)
        half_j = sb("half_j", [P, PER_TOKEN], U32)
        half_f = sb("half_f", [P, PER_TOKEN])
        picked = sb("picked", [P, 2, PER_TOKEN])
        gate_e = sb("gate_e", [P, R_H, TOPK])
        gate_n = sb("gate_n", [P, R_H])
        experts = sb("experts", [P, 3, PER_TOKEN], U32)
        gates = sb("gates", [P, 3, PER_TOKEN])
        products = sb("products", [P, D], BF16)
        u_index = sb("u_index", [P, 2, RING], U32)
        v_index = sb("v_index", [P, 2, RING], U32)
        dots = sb("dots", [P, 2, G])
        gelu = sb("gelu", [P, 2, G])
        weight = sb("weight", [P, 2, G])
        diag = sb("diag", [P, 2, G, P])
        qkv = arena[:, 0:2 * IN_W].rearrange("p (b n) -> p b n", b=2)
        probs = arena[:, 3584:5120].rearrange("p (a i n) -> p a i n", a=2, i=2)
        pT = arena[:, 5120:5888].rearrange("p (i n) -> p i n", i=2)
        fy = arena[:, 5888:6912].rearrange("p (b n) -> p b n", b=2)
        fT = arena[:, 6912:7424].rearrange("p (g n) -> p g n", g=2)
        squares = arena[:, 3584:3584 + RMS_HEADS * HD]
        turned = arena[:, 3584 + 640:3584 + 1280]
        turned2 = arena[:, 3584 + 1280:3584 + 1920]
        gate_b = arena[:, 5120:5120 + D].rearrange("p (a n) -> p a n", a=2)
        z = arena[:, 6144:6144 + D]
        scores = arena[:, 0:2 * 2048].rearrange("p (b n) -> p b n", b=2)
        cand = arena[:, 4096:6144]
        qpT = arena[:, 6144:6144 + 1024].rearrange("p (a i n) -> p a i n", a=2, i=2)

        def const(name):
            a, b = CONST[name]
            return consts[:, a:b]

        ident = const("ident")
        ones = const("ones")
        rope = const("rope").rearrange("p (b f n) -> p b f n", b=2, f=2)
        dft_ctx = const("dft_ctx").rearrange("p (f n) -> p f n", f=2)
        dft_lat = const("dft_lat").rearrange("p (b f n) -> p b f n", b=2, f=2)
        dft_ch = const("dft_ch")
        window = const("window")
        iota = const("iota")

        acc = ctx.enter_context(nc.psum_tensor("acc", [P, 2, 512], F32))
        pairs = [ctx.enter_context(nc.psum_tensor(f"pair{n}", [P, 2, 512], F32)) for n in range(PAIRS)]

        consts_landed = sem("consts_landed")
        tables_landed = sem("tables_landed")
        cond_landed = sem("cond_landed")
        x_landed = [sem(f"x_landed{n}") for n in range(3)]
        w_landed = [sem(f"w_landed{n}") for n in range(WSLOTS + EARLY_SLOTS)]
        w_used = sem("w_used")
        gate_diag_ready = sem("gate_diag_ready")
        ln_rows_landed = sem("ln_rows_landed")
        ctx_landed = sem("ctx_landed")
        bias_landed = sem("bias_landed")
        kv_stored = sem("kv_stored")
        y_stored = sem("y_stored")
        filled = sem("filled")
        drained_by_act = sem("drained_by_act")
        drained_by_dve = sem("drained_by_dve")
        cond_exp = sem("cond_exp")
        b_mod_ready = sem("b_mod_ready")
        cond_ready = sem("cond_ready")
        squares_ready = sem("squares_ready")
        root_in_ready = sem("root_in_ready")
        root_ready = sem("root_ready")
        norm_ready = sem("norm_ready")
        neg_max_ready = sem("neg_max_ready")
        ln_done = sem("ln_done")
        best_ready = sem("best_ready")
        gate_exp = sem("gate_exp")
        route_ready = sem("route_ready")
        acc_drained = sem("acc_drained")
        index_copied = sem("index_copied")
        issue_granted = sem("issue_granted")
        u_landed = [sem(f"u_landed{n}") for n in range(RING)]
        v_landed = [sem(f"v_landed{n}") for n in range(RING)]
        u_used = sem("u_used")
        v_used = sem("v_used")
        gelu_ready = sem("gelu_ready")
        weight_ready = sem("weight_ready")
        diag_ready = sem("diag_ready")
        dve_chain = sem("dve_chain")
        act_chain = sem("act_chain")

        N_CONST_DMAS = 2

        def weight_slot(slot):
            if slot < WSLOTS:
                return wtiles[:, slot, :, :]
            ring, at = divmod(slot - WSLOTS, EARLY_SLOTS // 2)
            flat = (u_rows, v_rows)[ring][:, :, :].rearrange("p s d -> p (s d)")
            return flat[:, at * NC * TW:(at + 1) * NC * TW].rearrange("p (c n) -> p c n", n=TW)

        def pair(key):
            return pairs[ROUND[key] % PAIRS]

        def wait_filled(eng, key):
            if key[0] in BY_TILE:
                eng.wait_ge(w_used, TILES[last_tile(key)])
            else:
                eng.wait_ge(filled, FILLED[key])
            return pair(key)

        def wait_drained(eng, key):
            if key[0] in BY_DVE:
                eng.wait_ge(drained_by_dve, DRAINED_BY_DVE[key])
            else:
                eng.wait_ge(drained_by_act, DRAINED_BY_ACT[key])

        def turns_of(eng, q, h0, h1, turn, behind=0):
            base = q * GROUPS

            def one(h):
                n = base + h - behind
                turn(n // 2, n % 2)

            if h0 < h1 and (h0 - behind) % 2:
                one(h0)
                h0 += 1
            if h1 - h0 >= 2:
                start = (base + h0 - behind) // 2
                with eng.Fori(start, start + (h1 - h0) // 2) as p:
                    turn(p, 0)
                    turn(p, 1)
                h0 += (h1 - h0) // 2 * 2
            if h0 < h1:
                one(h0)

        block = ctx.enter_context(nc.Block())

        @block.sync
        def _(sp):
            sp.dma_start(cond[:, :, :], i["cond"]).then_inc(cond_landed, 16)

            def weights(key, src):
                n = TILES[key]
                slot = slot_of(n)
                if last_in_slot(n):
                    sp.wait_ge(w_used, last_in_slot(n))
                sp.dma_start(weight_slot(slot), src).then_inc(w_landed[slot], 16)
                return slot

            def cols(w, l, n):
                return w[l, :, n * TW:(n + 1) * TW].rearrange("(c p) n -> p c n", p=P)

            for step in SCHEDULE:
                kind, a = step[0], step[1:]
                if kind == "mod":
                    l, part, t = a
                    if t < D // TW:
                        weights(step, cols(i["w_mod"], l, part * (D // TW) + t))
                elif kind == "proj":
                    weights(step, cols(i["w_in"], MIXES[a[0]][0], a[1]))
                elif kind == "outp":
                    weights(step, cols(i["w_out"], MIXES[a[0]][0], a[1]))
                elif kind == "wq" and a[1] < R_H:
                    l = MIXES[a[0]][0]
                    slot = weights(step, cols(i["peer_wq"], l, a[1]))
                    if a[1] >= SK_SLOTS:
                        sp.wait_ge(w_used, TILES[("wq", a[0], a[1] - SK_SLOTS)])
                    elif a[0]:
                        sp.wait_ge(w_used, TILES[("wq", a[0] - 1, R_H - 1)])
                    sp.dma_start(sktiles[:, a[1] % SK_SLOTS, :, :], i["sub_keys"][l, :, 2 * a[1]:2 * a[1] + 2, :])\
                        .then_inc(w_landed[slot], 16)
                elif kind == "bias":
                    l = a[0]
                    if l:
                        wait_filled(sp, ("O", 2, 5))
                    sp.dma_start(kT[:, :, 2 * P:3 * P], i["ctx_kT"][l]).then_inc(ctx_landed, 16)
                    sp.dma_start(v_ctx[:, :], i["ctx_v"][l]).then_inc(ctx_landed, 16)
                    sp.wait_ge(ln_done, ln_before(step))
                    for row in range(4):
                        at = ROWS_MAX_DIFF - row
                        to = bias[row % 2 * GRID_W:(row % 2 + 1) * GRID_W, row // 2]
                        sp.dma_start(to.rearrange("p h (j c) -> p h j c", j=4), i["rpb"][l, :, :, at:at + 4, :]).then_inc(bias_landed, 16)
                elif kind in ("ln1", "ln2") and a[1] == 0:
                    which = 1 if kind == "ln1" else 2
                    n, l = LN[(a[0], which)], a[0] // 3
                    if n > 1:
                        sp.wait_ge(ln_done, n - 1)
                    if which == 1 and MIXES[mix_of(a[0])][1]:
                        wait_filled(sp, ("O", BLOCKS[mix_of(a[0])][-1], 5))
                    for r, name in enumerate((f"ln{which}_g", f"ln{which}_b")):
                        sp.dma_start(ln_rows[:, r, :], i[name][l, :].partition_broadcast(P))\
                            .then_inc(ln_rows_landed, 16)
                elif kind == "ln2" and a[0] >= 3:
                    sp.wait_ge(ln_done, LN[(a[0], 2)])
                    dst = o["y_prompt"][0] if a[0] == 3 else o["y_sample"][0, (a[0] - 4) * P:(a[0] - 3) * P]
                    sp.dma_start(dst, x_tok[:, a[0] % 3, :]).then_inc(y_stored, 16)
                elif kind == "kvout":
                    q = a[0]
                    l = q // 3
                    sp.wait_ge(norm_ready, NORM[q])
                    wait_drained(sp, ("J", mix_of(q), PROJ_ORDER[-1]))
                    for name, at, n in (("new_na_k", NA_K, 256), ("new_na_v", NA_V, 256),
                                        ("new_gqa_k", G_K, 128), ("new_gqa_v", G_V, 128)):
                        sp.dma_start(o[name][l], qkv[:, 0, at:at + n]).then_inc(kv_stored, 16)
            sp.wait_ge(kv_stored, 16 * 8)
            sp.wait_ge(y_stored, 16 * 3)

        @block.gpsimd
        def _(pool):
            def gather_u(turn, slot, half):
                pool.wait_ge(u_used, turn * RING + slot + 1)
                pool.sem_inc(issue_granted, 1)
                pool.indirect_dma_start(
                    out=u_rows[:, slot, :], out_offset=None, in_=i["peer_u"],
                    in_offset=bass.IndirectOffsetOnAxis(ap=u_index[:, half, slot:slot + 1], axis=0),
                ).then_inc(u_landed[slot], 16)

            def gather_v(turn, slot, half):
                pool.wait_ge(v_used, turn * RING + slot + 1)
                pool.sem_inc(issue_granted, 1)
                pool.indirect_dma_start(
                    out=v_rows[:, slot, :], out_offset=None, in_=i["peer_v"],
                    in_offset=bass.IndirectOffsetOnAxis(ap=v_index[:, half, slot:slot + 1], axis=0),
                ).then_inc(v_landed[slot], 16)

            RINGS = PER_TOKEN // RING

            def phase(q, n, half):
                first, last = type(n) is int and n == 0, type(n) is int and n == RINGS
                e = experts[:, q % 3, :]
                if not last:
                    pool.tensor_copy(u_index[:, half, :], e[:, bass.ds(n * RING, RING)]).then_inc(index_copied, 1)
                if not first:
                    pool.tensor_copy(v_index[:, half, :], e[:, bass.ds(n * RING - RING, RING)]).then_inc(index_copied, 1)
                pool.wait_ge(index_copied, q * 2 * RINGS + n * 2 + (0 if last else 1))
                for j in range(RING):
                    if not last:
                        gather_u(n + q * RINGS, j, half)
                    if not first:
                        gather_v(n + q * RINGS - 1, j, half)

            for q in range(6):
                pool.wait_ge(route_ready, ROUTE[q])
                if q == 0:
                    pool.wait_ge(w_used, EARLY_TILES)
                phase(q, 0, 0)
                with pool.Fori(1, RINGS - 1, 2) as n:
                    phase(q, n, 1)
                    phase(q, n + 1, 0)
                phase(q, RINGS - 1, 1)
                phase(q, RINGS, 0)

        @block.tensor
        def _(pe):
            def open_round(key):
                if ROUND[key] >= PAIRS:
                    wait_drained(pe, ROUNDS[ROUND[key] - PAIRS])
                return pair(key)

            def tile(key):
                slot, n = tile_arrival(key)
                pe.wait_ge(w_landed[slot], n)
                return weight_slot(slot)

            def transpose8(dst, src):
                for c in range(NC):
                    last = nc.tensor.transpose(dst[:, c // 4, (c % 4) * P:(c % 4 + 1) * P], src(c), ident)
                return last

            def scores_round(q, u):
                m, b = mix_of(q), place_in_mix(q)
                nk = 3 * P if MIXES[m][1] else P
                dst = open_round(("A", q, u))
                kp = min(u, 2)
                for h in range(2):
                    rows = slice(64 * h, 64 * h + 64)
                    last = nc.tensor.matmul(dst[:, h, 0:nk], qT[rows, u, b * P:(b + 1) * P], kT[rows, kp, 0:nk],
                                            start=True, stop=True)
                last.then_inc(filled, 1)

            def attention(m, n):
                latent = MIXES[m][1]
                chunks = 3 if latent else 1
                out_of, probs_of, scores_of = units_of(m, n)
                if n == 0:
                    wait_drained(pe, ("T1", BLOCKS[m][-1]))
                    if latent:
                        pe.wait_ge(ctx_landed, 32 * (MIXES[m][0] + 1))
                if out_of:
                    q, u = out_of
                    b = place_in_mix(q)
                    dst = open_round(("O", q, u))
                    wait_drained(pe, ("PT", q, u))
                    for h in range(2):
                        own = (NA_V + (2 * u + h) * HD) if u < 2 else (G_V + h * HD)
                        old = ((2 * u + h) * HD) if u < 2 else (256 + h * HD)
                        for k in range(chunks):
                            v = v_ctx[:, old:old + HD] if k == 2 else qkv[:, k, own:own + HD]
                            last = nc.tensor.matmul(dst[:, 0, h * HD:(h + 1) * HD], pT[:, h, k * P:(k + 1) * P], v,
                                                    start=(k == 0), stop=(k == chunks - 1))
                    last.then_inc(filled, 1)
                if probs_of:
                    q, u = probs_of
                    dst = open_round(("PT", q, u))
                    wait_drained(pe, ("A", q, u))
                    for h in range(2):
                        for k in range(chunks):
                            last = nc.tensor.transpose(dst[:, h, k * P:(k + 1) * P], probs[:, u % 2, h, k * P:(k + 1) * P], ident)
                    last.then_inc(filled, 1)
                if scores_of:
                    scores_round(*scores_of)

            def fourier(m, part):
                l, latent = MIXES[m]
                qs = BLOCKS[m]
                t = width(m)
                if part == 0:
                    wait_drained(pe, ("T1", qs[-1]))
                    for b, q in enumerate(qs):
                        dst = open_round(("FY", q))
                        for g in range(2):
                            last = nc.tensor.matmul(dst[:, 0, g * 256:(g + 1) * 256], hT[:, g, b * P:(b + 1) * P], dft_ch,
                                                    start=True, stop=True)
                        last.then_inc(filled, 1)
                elif part == 1:
                    dst = open_round(("FF", m))
                    wait_drained(pe, ("FY", qs[-1]))
                    for g in range(2):
                        for b in range(len(qs)):
                            for f in range(2):
                                table = dft_lat[:, b, f, :] if latent else dft_ctx[:, f, :]
                                last = nc.tensor.matmul(dst[:, g, 0:t], fy[:, b, g * 256 + f * P:g * 256 + (f + 1) * P], table,
                                                        start=(b == 0 and f == 0), stop=(b == len(qs) - 1 and f == 1))
                    last.then_inc(filled, 1)
                else:
                    pe.wait_ge(tables_landed, 32)
                    for b, q in enumerate(qs):
                        dst = open_round(("FO", q))
                        wait_drained(pe, ("FF", m))
                        for g in range(2):
                            last = nc.tensor.matmul(dst[:, 0, g * P:(g + 1) * P], fT[:, g, b * P:(b + 1) * P], wf[:, l, g, :],
                                                    start=True, stop=True)
                        last.then_inc(filled, 1)

            def experts_sum(q, h0, h1):
                if h0 == 0 and q == 0:
                    pe.sem_inc(v_used, RING)

                def turn(pairs_before, half):
                    for j in range(G):
                        slot = half * G + j
                        pe.wait_ge(diag_ready, pairs_before * RING + slot + 1)
                        pe.wait_ge(v_landed[slot], pairs_before * 16 + 16)
                        for n in range(2):
                            last = nc.tensor.matmul(acc[:, n, :], diag[:, half, j, :], v_rows[:, slot, n * 512:(n + 1) * 512],
                                                    start=False, stop=True, skip_group_check=True)
                        last.then_inc(v_used, 1)

                if h0 <= 2 < h1:
                    if q:
                        pe.wait_ge(acc_drained, q)
                    for n in range(2):
                        nc.tensor.matmul(acc[:, n, :], const("zero")[0:1, :], consts[0:1, 0:512], start=True, stop=True)
                turns_of(pe, q, max(h0, 2), h1, turn, behind=2)

            pe.wait_ge(cond_ready, 1)
            for step in SCHEDULE:
                kind, a = step[0], step[1:]
                if kind == "gather":
                    experts_sum(*a)
                elif kind == "mod":
                    l, part, t = a
                    if t < D // TW:
                        dst = open_round(("MR",) + a)
                        w = tile(step)
                        for k in range(NC):
                            at = QUADRANT * (k % GROUPS_OF_PE)
                            last = nc.tensor.matmul(dst[at:at + QUADRANT, 0, 0:TW], cond_s[:, k, :], w[:, k, :],
                                                    start=(k < GROUPS_OF_PE), stop=(k >= NC - GROUPS_OF_PE),
                                                    tile_position=(0, at))
                        last.then_inc(w_used, 1)
                    if t:
                        dst = open_round(("MC", l, part, t - 1))
                        wait_drained(pe, ("MR", l, part, t - 1))
                        if step == ("mod", 0, 0, 1):
                            pe.wait_ge(consts_landed, 16 * N_CONST_DMAS)
                        for k in range(TW // P):
                            last = nc.tensor.matmul(dst[:, 0, 2 * k:2 * k + 2], mod_row[:, (t - 1) % 2, k * P:(k + 1) * P],
                                                    const("halves"), start=True, stop=True)
                        last.then_inc(filled, 1)
                elif kind == "xT":
                    q = a[0]
                    dst = open_round(("X", q))
                    if q < 3:
                        pe.wait_ge(x_landed[q], 16)
                    else:
                        pe.wait_ge(ln_done, LN[(q - 3, 2)])
                    transpose8(dst, lambda c: x_tok[:, q % 3, c * P:(c + 1) * P]).then_inc(filled, 1)
                elif kind in ("proj", "outp"):
                    m, n = a
                    w = tile(step)
                    if n == (PROJ_ORDER[0] if kind == "proj" else 0):
                        for q in BLOCKS[m]:
                            wait_drained(pe, ("X" if kind == "proj" else "OT", q))
                    if kind == "proj":
                        both = open_round(("J", m, n))
                    for b, q in enumerate(BLOCKS[m]):
                        if kind == "outp":
                            dst = open_round(("Z", q)) if n == 0 else pair(("Z", q))
                            dst = dst[:, n // 2, (n % 2) * TW:(n % 2 + 1) * TW]
                        else:
                            dst = both[:, b, 0:TW]
                        for k in range(NC):
                            last = nc.tensor.matmul(dst, hT[:, k, b * P:(b + 1) * P], w[:, k, :],
                                                    start=(k == 0), stop=(k == NC - 1))
                    last.then_inc(w_used, 1)
                elif kind == "qkT":
                    q = a[0]
                    b = place_in_mix(q)
                    src = qkv[:, b, :]
                    dst = open_round(("T0", q))
                    pe.wait_ge(norm_ready, NORM[q])
                    wait_drained(pe, ("J", mix_of(q), PROJ_ORDER[-1]))
                    parts = [src[:, NA_Q + k * P:NA_Q + (k + 1) * P] for k in range(2)]
                    parts += [src[:, G_Q + k * P:G_Q + (k + 1) * P] for k in range(4)]
                    parts += [src[:, NA_K + k * P:NA_K + (k + 1) * P] for k in range(2)]
                    transpose8(dst, lambda c: parts[c]).then_inc(filled, 1)
                    dst = open_round(("T1", q))
                    for k, at in enumerate((G_K, FN, FN + P)):
                        last = nc.tensor.transpose(dst[:, 0, k * P:(k + 1) * P], src[:, at:at + P], ident)
                    last.then_inc(filled, 1)
                elif kind == "att":
                    attention(*a)
                elif kind == "four":
                    fourier(*a)
                elif kind == "oT":
                    q = a[0]
                    b = place_in_mix(q)
                    dst = open_round(("OT", q))
                    wait_drained(pe, ("O", q, 5))
                    wait_drained(pe, ("FO", q))
                    at = [NA_Q, NA_Q + P, G_Q, G_Q + P, G_Q + 2 * P, G_Q + 3 * P, FN, FN + P]
                    transpose8(dst, lambda c: qkv[:, b, at[c]:at[c] + P]).then_inc(filled, 1)
                elif kind in ("gate", "gate2"):
                    q, which = (BLOCKS[a[0]][0], 1) if kind == "gate" else (a[0], 2)
                    dst = open_round(("G", q, which))
                    pe.wait_ge(gate_diag_ready, GATE[(q, which)])
                    for n in range(2):
                        last = nc.tensor.matmul(dst[:, n, :], ones, z[:, n * 512:(n + 1) * 512], start=True, stop=True)
                    last.then_inc(filled, 1)
                elif kind == "h2":
                    q, part = a
                    b = place_in_mix(q)
                    if part == 0:
                        dst = open_round(("X2", q))
                        pe.wait_ge(ln_done, LN[(q, 1)])
                        transpose8(dst, lambda c: x_tok[:, q % 3, c * P:(c + 1) * P]).then_inc(filled, 1)
                    else:
                        dst = open_round(("H2", q))
                        wait_drained(pe, ("X2", q))
                        transpose8(dst, lambda c: hT[:, c, b * P:(b + 1) * P]).then_inc(filled, 1)
                elif kind == "wq":
                    m, n = a
                    t = width(m)
                    if n < R_H:
                        dst = open_round(("WQ", m, n))
                        w = tile(step)
                        for h in range(2):
                            for k in range(NC):
                                last = nc.tensor.matmul(dst[:, h, 0:t], w[:, k, h * P:(h + 1) * P], hT[:, k, 0:t],
                                                        start=(k == 0), stop=(k == NC - 1))
                        last.then_inc(filled, 1)
                    if n:
                        dst = open_round(("SC", m, n - 1))
                        wait_drained(pe, ("WQ", m, n - 1))
                        for b in range(len(BLOCKS[m])):
                            for h in range(2):
                                last = nc.tensor.matmul(dst[:, b, h * P:(h + 1) * P], qpT[:, (n - 1) % 2, h, b * P:(b + 1) * P],
                                                        sktiles[:, (n - 1) % SK_SLOTS, h, :], start=True, stop=True)
                        last.then_inc(w_used, 1)

        @block.scalar
        def _(act):
            def drain(key, ops):
                for out, src in ops:
                    last = nc.scalar.copy(out, src)
                last.then_inc(drained_by_act, 1)

            def chunks(dst):
                return dst[:, :, :].rearrange("p a (c n) -> p (a c) n", n=P)

            def modulate(key, q, half):
                l, latent = q // 3, int(q % 3 > 0)
                b = place_in_mix(q)
                dst = wait_filled(act, key)
                for part in ((PART_SH1, PART_SC1), (PART_SH2, PART_SC2))[half]:
                    wait_drained(act, ("MC", l, part, D // TW - 1))
                for c in range(NC):
                    last = nc.scalar.activation(hT[:, c, b * P:(b + 1) * P], chunks(dst)[:, c, :], ACT.Identity,
                                                bias=mod_cols[:, l, 3 * half, c, latent:latent + 1],
                                                scale=mod_cols[:, l, 3 * half + 1, c, latent:latent + 1])
                last.then_inc(drained_by_act, 1)

            def square_root(key):
                n = RMS_HEADS if key[0] == "norm" else 1
                act.wait_ge(root_in_ready, ROOTS[key])
                nc.scalar.activation(root[:, 0:n], root_in[:, 0:n], ACT.Sqrt).then_inc(root_ready, 1)

            def exponentials(q, u):
                nk = 3 * P if MIXES[mix_of(q)][1] else P
                dst = wait_filled(act, ("A", q, u))
                act.wait_ge(neg_max_ready, UNIT[(q, u)])
                for h in range(2):
                    last = nc.scalar.activation(probs[:, u % 2, h, 0:nk], dst[:, h, 0:nk], ACT.Exp,
                                                bias=neg_max[:, u % 2, h:h + 1], scale=SCALE,
                                                accum_out=row_sum[:, u % 2, h:h + 1])
                last.then_inc(drained_by_act, 1)

            def attention(m, n):
                nk = 3 * P if MIXES[m][1] else P
                _, probs_of, scores_of = units_of(m, n)
                if probs_of:
                    key = ("PT",) + probs_of
                    dst = wait_filled(act, key)
                    drain(key, [(pT[:, :, 0:nk], dst[:, :, 0:nk])])
                if scores_of:
                    exponentials(*scores_of)

            def expert_weights(q, h0, h1):
                def diagonals(p, half):
                    act.wait_ge(weight_ready, p * 2 + half + 1)
                    for j in range(G):
                        act.wait_ge(v_used, p * RING + half * G + j + 1)
                        nc.scalar.activation(diag[:, half, j, :], ident, ACT.Copy, scale=weight[:, half, j:j + 1])\
                            .then_inc(diag_ready, 1)

                def gelus(p, half):
                    act.wait_ge(u_used, p * RING + (half + 1) * G + RING)
                    nc.scalar.activation(gelu[:, half, :], dots[:, half, :], ACT.Gelu).then_inc(gelu_ready, 1)

                def turn(p, half):
                    diagonals(p - 1 if half == 0 else p, 1 - half)
                    gelus(p, half)

                base = q * GROUPS
                if h0 == 0:
                    gelus(base // 2, 0)
                turns_of(act, q, max(h0, 1), min(h1, GROUPS), turn)
                if h0 <= GROUPS < h1:
                    diagonals((base + GROUPS - 1) // 2, 1)

            act.dma_start(consts[:, :], i["consts"]).then_inc(consts_landed, 16)
            act.dma_start(x_tok[:, 0, :], i["x_prompt"][0]).then_inc(x_landed[0], 16)
            act.dma_start(b_mod[:, :, :, :], i["b_mod"]).then_inc(consts_landed, 16)
            act.dma_start(gains[:, :, :, :], i["gains"].partition_broadcast(P)).then_inc(tables_landed, 16)
            act.dma_start(wf[:, :, :, :], i["wf"]).then_inc(tables_landed, 16)
            act.wait_ge(cond_landed, 16)
            nc.scalar.activation(cond_e[:, :, :], cond[:, :, :], ACT.Exp, scale=-1.0).then_inc(cond_exp, 1)
            for step in SCHEDULE:
                kind, a = step[0], step[1:]
                if kind == "gather":
                    expert_weights(*a)
                elif kind == "mod":
                    if a[2] < D // TW:
                        key = ("MR",) + a
                        dst = wait_filled(act, key)
                        drain(key, [(mod_row[:, a[2] % 2, :], dst[:, 0, 0:TW])])
                    if a[2]:
                        l, part, t = a
                        key = ("MC", l, part, t - 1)
                        dst = wait_filled(act, key)
                        if key == ("MC", 0, 0, 0):
                            act.wait_ge(b_mod_ready, 1)
                        for k in range(TW // P):
                            c = (t - 1) * TW // P + k
                            last = nc.scalar.activation(mod_cols[:, l, part, c, :], dst[:, 0, 2 * k:2 * k + 2], ACT.Identity,
                                                        bias=b_mod[:, l, part, c:c + 1])
                        last.then_inc(drained_by_act, 1)
                    if step == ("mod", 0, 0, 0):
                        act.wait_ge(consts_landed, 16 * N_CONST_DMAS)
                elif kind == "xT":
                    modulate(("X", a[0]), a[0], 0)
                    if a[0] == 0:
                        for b in range(2):
                            act.dma_start(x_tok[:, b + 1, :], i["x_sample"][0, b * P:(b + 1) * P]).then_inc(x_landed[b + 1], 16)
                elif kind == "proj":
                    m, n = a
                    nb = len(BLOCKS[m])
                    if n == PROJ_ORDER[0] and m:
                        act.wait_ge(route_ready, routes_before(step))
                        if ln_before(step):
                            act.wait_ge(ln_done, ln_before(step))
                        if m == 2:
                            act.wait_ge(kv_stored, 64)
                    dst = wait_filled(act, ("J", m, n))
                    drain(("J", m, n), [(qkv[:, 0:nb, n * TW:(n + 1) * TW], dst[:, 0:nb, 0:TW])])
                elif kind == "norm":
                    q = a[0]
                    wait_drained(act, ("J", mix_of(q), TO_NORM[-1]))
                    if NORM[q] > 1:
                        act.wait_ge(norm_ready, NORM[q] - 1)
                    nc.scalar.activation(squares, qkv[:, place_in_mix(q), G_Q:G_V], ACT.Square).then_inc(squares_ready, 1)
                    square_root(("norm", q))
                elif kind == "qkT":
                    q = a[0]
                    at = slice(place_in_mix(q) * P, (place_in_mix(q) + 1) * P)
                    dst = chunks(wait_filled(act, ("T0", q)))
                    drain(("T0", q), [(qT[:, :, at], dst[:, 0:6, :]), (kT[:, 0:2, at], dst[:, 6:8, :])])
                    dst = chunks(wait_filled(act, ("T1", q)))
                    drain(("T1", q), [(kT[:, 2, at], dst[:, 0, :]), (hT[:, 0:2, at], dst[:, 1:3, :])])
                elif kind == "att":
                    attention(*a)
                elif kind == "four":
                    m, part = a
                    if part == 0:
                        for b, q in enumerate(BLOCKS[m]):
                            dst = wait_filled(act, ("FY", q))
                            drain(("FY", q), [(fy[:, b, :], dst[:, 0, :])])
                    elif part == 1:
                        dst = wait_filled(act, ("FF", m))
                        drain(("FF", m), [(fT[:, :, 0:width(m)], dst[:, :, 0:width(m)])])
                    else:
                        for b, q in enumerate(BLOCKS[m]):
                            dst = wait_filled(act, ("FO", q))
                            drain(("FO", q), [(qkv[:, b, FN:IN_W], dst[:, 0, 0:IN_W - FN])])
                elif kind == "oT":
                    q = a[0]
                    at = slice(place_in_mix(q) * P, (place_in_mix(q) + 1) * P)
                    dst = wait_filled(act, ("OT", q))
                    drain(("OT", q), [(hT[:, :, at], chunks(dst))])
                elif kind in ("gate", "gate2"):
                    key = ("G", BLOCKS[a[0]][0], 1) if kind == "gate" else ("G", a[0], 2)
                    if ln_before(step):
                        act.wait_ge(ln_done, ln_before(step))
                    if routes_before(step):
                        act.wait_ge(route_ready, routes_before(step))
                    dst = wait_filled(act, key)
                    drain(key, [(gate_b, dst[:, :, :])])
                elif kind in ("ln1", "ln2") and a[1] == 0:
                    square_root((kind, a[0]))
                elif kind == "h2":
                    q, part = a
                    if part == 0:
                        modulate(("X2", q), q, 1)
                    else:
                        if q >= 3:
                            act.wait_ge(ln_done, LN[(q - 3, 2)])
                        dst = wait_filled(act, ("H2", q))
                        drain(("H2", q), [(h_tok[:, q % 3, :].rearrange("p (a n) -> p a n", a=2), dst[:, :, :])])
                elif kind == "wq":
                    m, n = a
                    nb, t = len(BLOCKS[m]), width(m)
                    if n < R_H:
                        dst = wait_filled(act, ("WQ", m, n))
                        drain(("WQ", m, n), [(qpT[:, n % 2, :, 0:t], dst[:, :, 0:t])])
                    if n == 1:
                        act.wait_ge(ln_done, ln_before(step))
                        if not MIXES[m][1]:
                            act.wait_ge(kv_stored, 64 * (MIXES[m][0] + 1))
                    if n:
                        dst = wait_filled(act, ("SC", m, n - 1))
                        drain(("SC", m, n - 1), [(scores[:, 0:nb, (n - 1) * TW:n * TW], dst[:, 0:nb, 0:TW])])
                elif kind == "pick" and a[1] == 4:
                    act.wait_ge(best_ready, ROUTE[a[0]])
                    nc.scalar.activation(gate_e[:, :, :], gate_e[:, :, :], ACT.Exp).then_inc(gate_exp, 1)

        @block.vector
        def _(dve):
            links = [0]

            def link(ins):
                links[0] += 1
                ins.then_inc(dve_chain, 1)
                dve.wait_ge(dve_chain, links[0])

            def spread(ap, shape):
                return ap.to_broadcast(shape)

            def maxima(q, u):
                m, b = mix_of(q), place_in_mix(q)
                nk = 3 * P if MIXES[m][1] else P
                dst = wait_filled(dve, ("A", q, u))
                if MIXES[m][1] and u < 2:
                    link(nc.vector.tensor_tensor(dst[:, :, 0:2 * P], dst[:, :, 0:2 * P], bias[:, b, 2 * u:2 * u + 2, :], ALU.add))
                link(nc.vector.reduce_max(maxes[:, :], dst[:, :, 0:nk], AX.X))
                nc.vector.tensor_scalar(neg_max[:, u % 2, :], maxes[:, :], -SCALE, None, ALU.mult).then_inc(neg_max_ready, 1)
                dve.wait_ge(neg_max_ready, UNIT[(q, u)])

            def attention(m, n):
                out_of, _, scores_of = units_of(m, n)
                if out_of:
                    q, u = out_of
                    b = place_in_mix(q)
                    wait_drained(dve, ("A", q, u))
                    link(nc.vector.reciprocal(inv_sum[:, :], row_sum[:, u % 2, :]))
                    dst = wait_filled(dve, ("O", q, u))
                    if u < 2:
                        out = qkv[:, b, 2 * u * HD:(2 * u + 2) * HD].rearrange("p (i d) -> p i d", i=2)
                    else:
                        out = qkv[:, b, G_Q:G_Q + Q_H * HD].rearrange("p (g i d) -> p i g d", g=2, i=4)[:, u - 2]
                    nc.vector.tensor_tensor(out, dst[:, 0, 0:2 * HD].rearrange("p (i d) -> p i d", i=2),
                                            spread(inv_sum[:, :].unsqueeze(2), [P, 2, HD]), ALU.mult)\
                        .then_inc(drained_by_dve, 1)
                    wait_drained(dve, ("O", q, u))
                if scores_of:
                    maxima(*scores_of)

            def layer_norm(q, which, part):
                slot, l = q % 3, q // 3
                x = x_tok[:, slot, :]
                key = (q, which)
                if part == 0:
                    zz = z.rearrange("p (a n) -> p a n", a=2)
                    wait_drained(dve, ("G", BLOCKS[mix_of(q)][0] if which == 1 else q, which))
                    if which == 1:
                        dst = wait_filled(dve, ("Z", q))
                        if l == 0:
                            dve.wait_ge(x_landed[q], 16)
                        nc.vector.tensor_tensor(zz, dst[:, :, :], gate_b, ALU.mult).then_inc(drained_by_dve, 1)
                        wait_drained(dve, ("Z", q))
                    else:
                        dve.wait_ge(v_used, RING + PER_TOKEN * (q + 1))
                        nc.vector.tensor_tensor(zz, acc[:, :, :], gate_b, ALU.mult).then_inc(acc_drained, 1)
                        dve.wait_ge(acc_drained, q + 1)
                    link(nc.vector.scalar_tensor_tensor(out=z, in0=x, scalar=ALPHA, in1=z, op0=ALU.mult, op1=ALU.add))
                    nc.vector.bn_stats(stats[:, 0, :], z[:, 0:512])
                    link(nc.vector.bn_stats(stats[:, 1, :], z[:, 512:D]))
                    link(nc.vector.bn_aggr(mean_var[:, :], stats[:, :, :]))
                    nc.vector.tensor_scalar(root_in[:, 0:1], mean_var[:, 1:2], LN_EPS, None, ALU.add).then_inc(root_in_ready, 1)
                    return
                dve.wait_ge(root_ready, ROOTS[("ln1" if which == 1 else "ln2", q)])
                link(nc.vector.reciprocal(rroot[:, 0:1], root[:, 0:1]))
                link(nc.vector.tensor_scalar(z, z, mean_var[:, 0:1], rroot[:, 0:1], ALU.subtract, ALU.mult))
                dve.wait_ge(ln_rows_landed, 32 * LN[key])
                link(nc.vector.tensor_tensor(z, z, ln_rows[:, 0, :], ALU.mult))
                nc.vector.tensor_tensor(x, z, ln_rows[:, 1, :], ALU.add).then_inc(ln_done, 1)
                dve.wait_ge(ln_done, LN[key])

            def rms_norm_and_rotate(q):
                l, latent, b = q // 3, q % 3 > 0, place_in_mix(q)
                dve.wait_ge(squares_ready, NORM[q])
                link(nc.vector.reduce_sum(root_in[:, :], squares.rearrange("p (h d) -> p h d", d=HD), AX.X))
                nc.vector.tensor_scalar(root_in[:, :], root_in[:, :], 1.0 / HD, RMS_EPS, ALU.mult, ALU.add).then_inc(root_in_ready, 1)
                dve.wait_ge(root_ready, ROOTS[("norm", q)])
                link(nc.vector.reciprocal(rroot[:, :], root[:, :]))
                x = qkv[:, b, G_Q:G_V].rearrange("p (h d) -> p h d", d=HD)
                t1, t2, t3 = (t.rearrange("p (h d) -> p h d", d=HD) for t in (turned, turned2, squares))
                out = [x[:, 0:Q_H].rearrange("p (i g) d -> p g i d", g=KV_H), x[:, Q_H:]]

                def grouped(t):
                    return [t[:, 0:Q_H].rearrange("p (g i) d -> p g i d", g=KV_H), t[:, Q_H:]]

                dve.wait_ge(tables_landed, 32)
                link(nc.vector.tensor_tensor(t1, x, spread(rroot[:, :].unsqueeze(2), [P, RMS_HEADS, HD]), ALU.mult))
                by = [spread(gains[:, l, 0, :].unsqueeze(1), [P, Q_H, HD]), spread(gains[:, l, 1, :].unsqueeze(1), [P, KV_H, HD])]
                nc.vector.tensor_tensor(t1[:, 0:Q_H], t1[:, 0:Q_H], by[0], ALU.mult)
                link(nc.vector.tensor_tensor(t1[:, Q_H:], t1[:, Q_H:], by[1], ALU.mult))
                if latent:
                    nc.vector.tensor_tensor(t2, t1, spread(rope[:, b, 0, :].unsqueeze(1), [P, RMS_HEADS, HD]), ALU.mult)
                    for half in range(2):
                        for y in range(2):
                            to = slice(32 * half + 16 * y, 32 * half + 16 * y + 16)
                            of = slice(32 * half + 16 * (1 - y), 32 * half + 16 * (1 - y) + 16)
                            last = nc.vector.tensor_tensor(t3[:, :, to], t1[:, :, of],
                                                           spread(rope[:, b, 1, to].unsqueeze(1), [P, RMS_HEADS, 16]), ALU.mult)
                    link(last)
                    for d, s2, s3 in zip(out, grouped(t2), grouped(t3)):
                        last = nc.vector.tensor_tensor(d, s2, s3, ALU.add)
                else:
                    for d, s1 in zip(out, grouped(t1)):
                        last = nc.vector.tensor_copy(d, s1)
                last.then_inc(norm_ready, 1)

            def top_sixteen(groups):
                for v, out, _ in groups:
                    last = nc.vector.max(out=out[:, 0:8], in_=v)
                link(last)
                for v, out, at in groups:
                    last = nc.vector.max_index(out=at[:, 0:8], in_max=out[:, 0:8], in_values=v)
                link(last)
                for v, out, _ in groups:
                    last = nc.vector.match_replace(out=v, in_to_replace=out[:, 0:8], in_values=v, imm_value=LOWEST)
                link(last)
                for v, out, _ in groups:
                    last = nc.vector.max(out=out[:, 8:16], in_=v)
                link(last)
                for v, out, at in groups:
                    last = nc.vector.max_index(out=at[:, 8:16], in_max=out[:, 8:16], in_values=v)
                link(last)

            def pick_experts(q, part):
                l, slot = q // 3, q % 3
                c4 = cand.rearrange("p (h a b) -> p h a b", h=R_H, a=TOPK)
                top4 = top_s[:, :, :].rearrange("p (h f) k -> p h f k", f=2)
                shape = [P, R_H, TOPK, TOPK]
                top_f = scores[:, place_in_mix(q), 0:2 * R_H * TOPK].rearrange("p (h f k) -> p h f k", f=2, k=TOPK)
                if part < 4:
                    heads = slice(2 * part, 2 * part + 2)
                    two = [P, 2, TOPK, TOPK]
                    link(nc.vector.tensor_tensor(c4[:, heads], spread(top4[:, heads, 0, :].unsqueeze(3), two),
                                                 spread(top4[:, heads, 1, :].unsqueeze(2), two), ALU.add))
                    flat = cand.rearrange("p (h n) -> p h n", h=R_H)
                    top_sixteen([(flat[:, h], best_s[:, h], best_j[:, h]) for h in (2 * part, 2 * part + 1)])
                if part == 3:
                    nc.vector.tensor_tensor(gate_e[:, :, :], best_s[:, :, :], spread(best_s[:, :, 0:1], [P, R_H, TOPK]),
                                            ALU.subtract).then_inc(best_ready, 1)
                    link(nc.vector.tensor_copy(top_f, top_i[:, :, :].rearrange("p (h f) k -> p h f k", f=2)))
                if part >= 4:
                    f = part - 4
                    j = best_j[:, :, :].rearrange("p h k -> p (h k)")
                    hit = cand.rearrange("p (n a) -> p n a", a=TOPK)
                    op, by = ((ALU.logical_shift_right, 4), (ALU.bitwise_and, 15))[f]
                    link(nc.vector.tensor_scalar(half_j[:, :], j, by, None, op))
                    link(nc.vector.tensor_copy(half_f[:, :], half_j[:, :]))
                    link(nc.vector.tensor_tensor(hit, spread(half_f[:, :].unsqueeze(2), [P, PER_TOKEN, TOPK]),
                                                 spread(iota.unsqueeze(1), [P, PER_TOKEN, TOPK]), ALU.is_equal))
                    link(nc.vector.tensor_tensor(c4, c4, spread(top_f[:, :, f, :].unsqueeze(2), shape), ALU.mult))
                    link(nc.vector.reduce_sum(picked[:, f, :], hit, AX.X))
                if part < 5:
                    return
                link(nc.vector.scalar_tensor_tensor(out=picked[:, 0, :], in0=picked[:, 0, :], scalar=float(KEYS),
                                                    in1=picked[:, 1, :], op0=ALU.mult, op1=ALU.add))
                link(nc.vector.tensor_scalar(experts[:, slot, :], picked[:, 0, :], float(l * EXPERTS), None, ALU.add))
                dve.wait_ge(gate_exp, ROUTE[q])
                link(nc.vector.reduce_sum(gate_n[:, :], gate_e[:, :, :], AX.X))
                link(nc.vector.reciprocal(gate_n[:, :], gate_n[:, :]))
                nc.vector.tensor_tensor(gates[:, slot, :].rearrange("p (h k) -> p h k", h=R_H), gate_e[:, :, :],
                                        spread(gate_n[:, :].unsqueeze(2), [P, R_H, TOPK]), ALU.mult).then_inc(route_ready, 1)
                dve.wait_ge(route_ready, ROUTE[q])

            def gate_on_diagonals(key):
                q, which = key
                part = PART_G1 if which == 1 else PART_G2
                wait_drained(dve, ("MC", q // 3, part, D // TW - 1))
                wait_filled(dve, ROUNDS[ROUND[("G", q, which)] - 1])
                column = mod_cols[:, q // 3, part, :, int(q % 3 > 0)]
                nc.vector.tensor_tensor(z.rearrange("p (c n) -> p c n", c=NC), spread(ident.unsqueeze(1), [P, NC, P]),
                                        spread(column.unsqueeze(2), [P, NC, P]), ALU.mult).then_inc(gate_diag_ready, 1)

            def expert_dots(q, h0, h1):
                slot_q = q % 3
                if h0 == 0:
                    wait_drained(dve, ("H2", q))
                    if q == 0:
                        dve.sem_inc(u_used, RING)

                def weigh(p, half, at):
                    dve.wait_ge(gelu_ready, p * 2 + half + 1)
                    nc.vector.tensor_tensor(weight[:, half, :], gelu[:, half, :], gates[:, slot_q, bass.ds(at, G)], ALU.mult)\
                        .then_inc(weight_ready, 1)

                def dot(p, half):
                    for j in range(G):
                        slot = half * G + j
                        dve.wait_ge(u_used, p * RING + slot + RING)
                        dve.wait_ge(u_landed[slot], p * 16 + 16)
                        nc.vector.tensor_tensor_reduce(out=products[:, :], in0=u_rows[:, slot, :], in1=h_tok[:, slot_q, :],
                                                       scale=1.0, scalar=0.0, op0=ALU.mult, op1=ALU.add,
                                                       accum_out=dots[:, half, j:j + 1]).then_inc(u_used, 1)

                first = q * GROUPS // 2

                def turn(p, half):
                    weigh(p - 1 if half == 0 else p, 1 - half, (p - first) * RING + half * G - G)
                    dot(p, half)

                if h0 == 0:
                    dot(first, 0)
                turns_of(dve, q, max(h0, 1), min(h1, GROUPS), turn)
                if h0 <= GROUPS < h1:
                    weigh(first + GROUPS // 2 - 1, 1, PER_TOKEN - G)

            dve.wait_ge(cond_landed, 16)
            dve.wait_ge(cond_exp, 1)
            link(nc.vector.tensor_scalar(cond_e[:, :, :], cond_e[:, :, :], 1.0, None, ALU.add))
            link(nc.vector.reciprocal(cond_e[:, :, :], cond_e[:, :, :]))
            link(nc.vector.memset(cond_s[:, :, :], 0.0))
            nc.vector.tensor_tensor(cond_s[:, :, 0:2], cond[:, :, :], cond_e[:, :, :], ALU.mult).then_inc(cond_ready, 1)
            dve.wait_ge(consts_landed, 16 * N_CONST_DMAS)
            scales = b_mod[:, :, :, :].rearrange("p l (h s) c -> p l h s c", s=3)[:, :, :, PART_SC1]
            nc.vector.tensor_scalar(scales, scales, 1.0, None, ALU.add).then_inc(b_mod_ready, 1)
            for step in SCHEDULE:
                kind, a = step[0], step[1:]
                if kind == "gather":
                    expert_dots(*a)
                elif kind == "bias":
                    dve.wait_ge(bias_landed, 64 * (a[0] + 1))
                    by_row = rows[:, :].rearrange("p (n c) -> p n c", c=GRID_W)
                    link(nc.vector.scalar_tensor_tensor(out=by_row, in0=by_row, scalar=1.0 / SCALE,
                                                        in1=spread(window.unsqueeze(1), [P, 2 * D // GRID_W, GRID_W]),
                                                        op0=ALU.mult, op1=ALU.add))
                elif kind == "norm":
                    rms_norm_and_rotate(a[0])
                elif kind == "att":
                    attention(*a)
                elif kind == "ln1":
                    layer_norm(a[0], 1, a[1])
                elif kind == "gate":
                    gate_on_diagonals((BLOCKS[a[0]][0], 1))
                elif kind == "gate2":
                    gate_on_diagonals((a[0], 2))
                elif kind == "ln2":
                    layer_norm(a[0], 2, a[1])
                elif kind == "top":
                    q, n = a
                    m, b = mix_of(q), place_in_mix(q)
                    wait_drained(dve, ("SC", m, 2 * n + 1))
                    top_sixteen([(scores[:, b, n * KEYS:(n + 1) * KEYS], top_s[:, n], top_i[:, n])
                                 for n in range(4 * n, 4 * n + 4)])
                elif kind == "pick":
                    pick_experts(*a)


def constants():
    import numpy as np

    def place(name, rows, value):
        a, b = CONST[name]
        out[rows, a:b] = np.asarray(value, np.float64).reshape(out[rows, a:b].shape).astype(np.float32)

    out = np.zeros((P, CONST_W), np.float32)
    place("ident", slice(None), np.eye(P))
    place("ones", slice(None), np.ones((P, P)))
    pos = np.arange(2 * P)
    inv = (1.0 / (np.float32(10000.0) ** (np.arange(16, dtype=np.float32) / np.float32(16)))).astype(np.float32)
    table = np.zeros((2 * P, 2, HD))
    for half, where in enumerate((pos // GRID_W, pos % GRID_W)):
        angle = (where.astype(np.float32)[:, None] * inv).astype(np.float64)
        at = 32 * half
        table[:, 0, at:at + 16] = table[:, 0, at + 16:at + 32] = np.cos(angle)
        table[:, 1, at:at + 16] = -np.sin(angle)
        table[:, 1, at + 16:at + 32] = np.sin(angle)
    place("rope", slice(None), table.reshape(2, P, 2 * HD).transpose(1, 0, 2))

    def dft(n):
        angle = 2 * np.pi * (np.outer(np.arange(n), np.arange(n)) % n) / n
        return np.stack([np.cos(angle), -np.sin(angle)]) / np.sqrt(n)

    place("dft_ctx", slice(None), dft(P).transpose(1, 0, 2))
    place("dft_lat", slice(None), dft(2 * P).reshape(2, 2, P, 2 * P).transpose(2, 1, 0, 3))
    channels = np.zeros((2, HD, 2, 2, HD))
    for g in range(2):
        channels[g, :, 0, g] = dft(HD)[0]
        channels[g, :, 1, g] = -dft(HD)[1]
    place("dft_ch", slice(None), channels.reshape(P, 2 * P))
    col = np.arange(GRID_W)
    start = np.clip(col - 8, 0, GRID_W - 16)
    inside = (col[None] >= start[:, None]) & (col[None] < start[:, None] + 16)
    place("window", slice(None), np.tile(np.where(inside, 0.0, -1e30), (2, 1)))
    place("halves", slice(None), np.tile(np.eye(QUADRANT)[:, :2], (GROUPS_OF_PE, 1)))
    place("iota", slice(None), np.tile(np.arange(TOPK), (P, 1)))
    return out


def bias_by_columns(rpb):
    import numpy as np

    out = np.zeros((DEPTH, GRID_W, NA_H, 2 * ROWS_MAX_DIFF + 1, GRID_W), rpb.dtype)
    first = NA_WIN_H - 1 - ROWS_MAX_DIFF
    for column in range(GRID_W):
        lo, hi = max(column - NA_WIN_W + 1, 0), min(column + NA_WIN_W, GRID_W)
        out[:, column, :, :, lo:hi] = rpb[:, :, first:first + 2 * ROWS_MAX_DIFF + 1,
                                          lo - column + NA_WIN_W - 1:hi - column + NA_WIN_W - 1]
    return out


def kernel(**inputs):
    import concourse.bacc as bacc
    import numpy as np
    from concourse.bass_utils import run_bass_kernel_spmd

    a = {k: np.asarray(v) for k, v in inputs.items()}
    n = DEPTH
    wf = np.zeros((2, HD, n, 2, 2, HD), np.float32)
    f = a["w_fourier"].reshape(n, 2, 2, HD, HD)
    for g in range(2):
        wf[g, :, :, :, g] = f[:, :, g].transpose(2, 0, 1, 3)

    def keys_by_channel(k):
        return k.transpose(0, 2, 3, 1).reshape(n, -1, P, P)

    arrays = {
        "x_prompt": a["x_prompt"], "x_sample": a["x_sample"], "consts": constants(),
        "cond": np.stack([a["c_ctx"], a["c"][0]]).reshape(2, NC, P).transpose(2, 1, 0),
        "rpb": bias_by_columns(a["na_rpb"]),
        "gains": np.stack([a["q_gain"], a["k_gain"]], axis=1),
        "wf": wf.reshape(P, n, 2, P),
        "w_mod": a["w_mod"], "b_mod": a["b_mod"].reshape(n, 6, NC, P).transpose(3, 0, 1, 2),
        "w_in": a["w_in"], "w_out": a["w_out"], "peer_wq": a["peer_wq"],
        "sub_keys": a["peer_subkeys"].transpose(0, 4, 1, 2, 3).reshape(n, P, 2 * R_H, KEYS),
        "ctx_kT": np.concatenate([keys_by_channel(a["cache_na_k"][0]), keys_by_channel(a["cache_gqa_k"][0])],
                                 axis=1).transpose(0, 2, 1, 3),
        "ctx_v": np.concatenate([a["cache_na_v"][0].reshape(n, P, -1), a["cache_gqa_v"][0].reshape(n, P, -1)], axis=2),
        "ln1_g": a["ln1_g"], "ln1_b": a["ln1_b"], "ln2_g": a["ln2_g"], "ln2_b": a["ln2_b"],
        "peer_u": a["peer_u"].reshape(n * EXPERTS, D), "peer_v": a["peer_v"].reshape(n * EXPERTS, D),
    }
    outs = {"y_prompt": (1, P, D), "y_sample": (1, 2 * P, D), "new_na_k": (n, P, 256), "new_na_v": (n, P, 256),
            "new_gqa_k": (n, P, 128), "new_gqa_v": (n, P, 128)}
    nc = bacc.Bacc("TRN2", target_bir_lowering=False, num_devices=1)
    arrays = {f"in_{k}": np.ascontiguousarray(v) for k, v in arrays.items()}
    i = {k[3:]: nc.dram_tensor(k, v.shape, mybir.dt.from_np(v.dtype), kind="ExternalInput").ap() for k, v in arrays.items()}
    o = {k: nc.dram_tensor(f"out_{k}", s, F32, kind="ExternalOutput").ap() for k, s in outs.items()}
    hybrid_step(nc, i, o)
    got = run_bass_kernel_spmd(nc, [arrays], core_ids=[0]).results[0]
    r = {k: got[f"out_{k}"] for k in outs}
    return (r["y_prompt"], r["y_sample"], r["new_na_k"].reshape(1, n, P, NA_H, HD), r["new_na_v"].reshape(1, n, P, NA_H, HD),
            r["new_gqa_k"].reshape(1, n, P, KV_H, HD), r["new_gqa_v"].reshape(1, n, P, KV_H, HD))
```
